# Optimizing a Trainium2 kernel written in Bass

```python
import jax, jax.numpy as jnp
from jax import lax
import numpy as np
import math
import jax
import jax.numpy as jnp

D_MODEL = 1024
BATCH = 1
SEQ = 256
DEPTH = 1

MLA_HEADS = 8
QK_NOPE_DIM = 64
QK_ROPE_DIM = 32
QK_HEAD_DIM = QK_NOPE_DIM + QK_ROPE_DIM
V_HEAD_DIM = 64
Q_LORA_RANK = 256
KV_LORA_RANK = 128
ROPE_THETA = 10000.0
Q_BLOCK = 128
MLA_OUT = MLA_HEADS * V_HEAD_DIM
MLA_IN = Q_LORA_RANK + KV_LORA_RANK + QK_ROPE_DIM

RWKV_HEADS = 8
RWKV_HEAD_DIM = 64
RWKV_DIM = RWKV_HEADS * RWKV_HEAD_DIM
DECAY_LORA = 64
ICLR_LORA = 64
VRES_LORA = 32
GATE_LORA = 128
RWKV_GN_EPS = 64e-5
RWKV_IN = 3 * RWKV_DIM + DECAY_LORA + ICLR_LORA + GATE_LORA

N_IN = MLA_IN + RWKV_IN
MIX_DIM = MLA_OUT + RWKV_DIM

N_EXPERTS = 32
TOP_K = 4
D_FF_EXPERT = D_MODEL
SWIGLU_LIMIT = 7.0
SWIGLU_ALPHA = 1.702
EXPERT_BLOCK = 128

DEEPNORM_ALPHA = (2 * DEPTH) ** 0.25
DEEPNORM_BETA = (8 * DEPTH) ** -0.25
LN_EPS = 1e-5
RMS_EPS = 1e-6


def layer_norm(x, g, b):
    xf = x.astype(jnp.float32)
    mu = xf.mean(-1, keepdims=True)
    var = jnp.square(xf - mu).mean(-1, keepdims=True)
    return ((xf - mu) * lax.rsqrt(var + LN_EPS) * g + b).astype(x.dtype)

def rms_norm(x, g):
    xf = x.astype(jnp.float32)
    return (xf * lax.rsqrt(jnp.square(xf).mean(-1, keepdims=True) + RMS_EPS) * g).astype(x.dtype)

def rope(x, cos, sin):
    xp = x.astype(jnp.float32).reshape(x.shape[:-1] + (x.shape[-1] // 2, 2))
    x0, x1 = xp[..., 0], xp[..., 1]
    out = jnp.stack([x0 * cos - x1 * sin, x0 * sin + x1 * cos], axis=-1)
    return out.reshape(x.shape).astype(x.dtype)

def causal_attention(q, k, v):
    b, s, h, dq = q.shape
    nb = s // Q_BLOCK
    scale = QK_HEAD_DIM ** -0.5
    q_blocks = jnp.moveaxis(q.reshape(b, nb, Q_BLOCK, h, dq), 1, 0)
    k_pos = jnp.arange(s)

    def one_block(args):
        qb, bi = args
        scores = jnp.einsum('bqhd,bkhd->bhqk', qb, k, preferred_element_type=jnp.float32) * scale
        q_pos = bi * Q_BLOCK + jnp.arange(Q_BLOCK)
        scores = jnp.where(k_pos[None, :] <= q_pos[:, None], scores, -jnp.inf)
        probs = jax.nn.softmax(scores, axis=-1).astype(v.dtype)
        return jnp.einsum('bhqk,bkhd->bqhd', probs, v)

    out = lax.map(one_block, (q_blocks, jnp.arange(nb)))
    return jnp.moveaxis(out, 0, 1).reshape(b, s, h, v.shape[-1])

def mla_group(p, cos, sin, q_norm_g, w_uq, kv_norm_g, w_uk, w_uv, out_g):
    b, s, _ = p.shape
    q_lat = p[..., :Q_LORA_RANK]
    kv_lat = p[..., Q_LORA_RANK:Q_LORA_RANK + KV_LORA_RANK]
    k_rot = p[..., Q_LORA_RANK + KV_LORA_RANK:]
    q = (rms_norm(q_lat, q_norm_g) @ w_uq).reshape(b, s, MLA_HEADS, QK_HEAD_DIM)
    q = jnp.concatenate([q[..., :QK_NOPE_DIM],
                         rope(q[..., QK_NOPE_DIM:], cos[:, :, None, :], sin[:, :, None, :])], axis=-1)
    c_kv = rms_norm(kv_lat, kv_norm_g)
    k_nope = (c_kv @ w_uk).reshape(b, s, MLA_HEADS, QK_NOPE_DIM)
    v = (c_kv @ w_uv).reshape(b, s, MLA_HEADS, V_HEAD_DIM)
    k_rot = rope(k_rot, cos, sin)
    k = jnp.concatenate([k_nope, jnp.broadcast_to(k_rot[:, :, None, :], (b, s, MLA_HEADS, QK_ROPE_DIM))], axis=-1)
    o = causal_attention(q, k, v)
    return rms_norm(o.reshape(b, s, MLA_OUT), out_g)

def rwkv7_recurrence(r, decay, k, v, kk, a):
    b, s, h, n = r.shape

    def step(state, inp):
        r_t, w_t, k_t, v_t, kk_t, a_t = inp
        sa = jnp.einsum('bhij,bhj->bhi', state, -kk_t)
        state = (state * w_t[:, :, None, :]
                 + sa[..., :, None] * (kk_t * a_t)[..., None, :]
                 + v_t[..., :, None] * k_t[..., None, :])
        return state, jnp.einsum('bhij,bhj->bhi', state, r_t)

    xs = tuple(jnp.moveaxis(z, 1, 0) for z in (r, decay, k, v, kk, a))
    _, out = lax.scan(step, jnp.zeros((b, h, n, n), jnp.float32), xs)
    return jnp.moveaxis(out, 0, 1)

def rwkv7_group(p, mu, w0, w2, a0, a2, g2, k_k, k_a, r_k, gn_g, gn_b, v_first, vres):
    b, s, _ = p.shape
    h_, n_ = RWKV_HEADS, RWKV_HEAD_DIM
    p_prev = jnp.pad(p[:, :-1], ((0, 0), (1, 0), (0, 0)))
    p = p + mu * (p_prev - p)
    c3 = 3 * RWKV_DIM
    r = p[..., :RWKV_DIM]
    k = p[..., RWKV_DIM:2 * RWKV_DIM]
    v = p[..., 2 * RWKV_DIM:c3]
    wd = p[..., c3:c3 + DECAY_LORA]
    ad = p[..., c3 + DECAY_LORA:c3 + DECAY_LORA + ICLR_LORA]
    gd = p[..., c3 + DECAY_LORA + ICLR_LORA:]
    w = -jax.nn.softplus(-(w0 + jnp.tanh(wd) @ w2).astype(jnp.float32)) - 0.5
    decay = jnp.exp(-jnp.exp(w))
    a = jax.nn.sigmoid(a0 + ad @ a2)
    g = jax.nn.sigmoid(gd) @ g2
    if vres is not None:
        v0, v1, v2 = vres
        v = v + (v_first - v) * jax.nn.sigmoid(v0 + (v @ v1) @ v2)
    heads = lambda z: z.reshape(b, s, h_, n_).astype(jnp.float32)
    r_h, k_h, v_h, a_h, d_h = heads(r), heads(k), heads(v), heads(a), heads(decay)
    kk = k_h * k_k.reshape(h_, n_)
    kk = kk / jnp.maximum(jnp.linalg.norm(kk, axis=-1, keepdims=True), 1e-12)
    k_h = k_h * (1.0 + (a_h - 1.0) * k_a.reshape(h_, n_))
    o = rwkv7_recurrence(r_h, d_h, k_h, v_h, kk, a_h)
    mean = o.mean(-1, keepdims=True)
    var = jnp.square(o - mean).mean(-1, keepdims=True)
    o = ((o - mean) * lax.rsqrt(var + RWKV_GN_EPS)).reshape(b, s, RWKV_DIM) * gn_g + gn_b
    bonus = jnp.sum(r_h * k_h * r_k, axis=-1, keepdims=True) * v_h
    o = (o + bonus.reshape(b, s, RWKV_DIM)) * g
    return o.astype(p.dtype), v

def clamped_swiglu(hh):
    x_glu = jnp.minimum(hh[..., ::2], SWIGLU_LIMIT)
    x_lin = jnp.clip(hh[..., 1::2], -SWIGLU_LIMIT, SWIGLU_LIMIT)
    return x_glu * jax.nn.sigmoid(SWIGLU_ALPHA * x_glu) * (x_lin + 1.0)

def moe_ffn(h, router_w, router_b, w1, b1, w2, b2):
    b, s, d = h.shape
    t = b * s
    ht = h.reshape(t, d)
    logits = (ht @ router_w + router_b).astype(jnp.float32)
    top_val, top_idx = lax.top_k(logits, TOP_K)
    gates = jax.nn.softmax(top_val, axis=-1)
    n_assign = t * TOP_K
    e_flat = top_idx.reshape(n_assign)
    tok_flat = jnp.arange(n_assign, dtype=jnp.int32) // TOP_K
    order = jnp.argsort(e_flat)
    e_sorted = e_flat[order]
    counts = jnp.bincount(e_flat, length=N_EXPERTS)
    starts = jnp.cumsum(counts) - counts
    padded = (counts + EXPERT_BLOCK - 1) // EXPERT_BLOCK * EXPERT_BLOCK
    pad_ends = jnp.cumsum(padded)
    pad_starts = pad_ends - padded
    dest = pad_starts[e_sorted] + (jnp.arange(n_assign) - starts[e_sorted])
    n_blocks = -(-n_assign // EXPERT_BLOCK) + N_EXPERTS
    n_slots = n_blocks * EXPERT_BLOCK
    slot_tok = jnp.full((n_slots,), t, jnp.int32).at[dest].set(tok_flat[order])
    slot_gate = jnp.zeros((n_slots,), jnp.float32).at[dest].set(gates.reshape(n_assign)[order])
    block_expert = jnp.minimum(
        jnp.searchsorted(pad_ends, jnp.arange(n_blocks) * EXPERT_BLOCK, side='right'), N_EXPERTS - 1)
    h_pad = jnp.concatenate([ht, jnp.zeros((1, d), ht.dtype)], axis=0)

    def expert_block(args):
        idx, e = args
        u = clamped_swiglu(h_pad[idx] @ w1[e] + b1[e])
        return u @ w2[e] + b2[e]

    y_slots = lax.map(expert_block, (slot_tok.reshape(n_blocks, EXPERT_BLOCK), block_expert))
    y = jnp.zeros((t + 1, d), jnp.float32).at[slot_tok].add(
        y_slots.reshape(n_slots, d).astype(jnp.float32) * slot_gate[:, None])
    return y[:t].reshape(b, s, d).astype(h.dtype)

def first_inputs(seed: int = 0) -> dict:
    key = jax.random.key(seed)
    keys = iter(jax.random.split(key, 64))

    def nrm(shape, scale):
        return jax.random.normal(next(keys), shape, jnp.float32) * scale

    L, D, C, E, F = DEPTH, D_MODEL, RWKV_DIM, N_EXPERTS, D_FF_EXPERT
    fan = D ** -0.5
    x = nrm((BATCH, SEQ, D), 1.0)
    c = nrm((BATCH, D), 1.0)
    positions = (jnp.arange(SEQ, dtype=jnp.int32)[None, :]
                 + jax.random.randint(next(keys), (BATCH, 1), 0, 2048, dtype=jnp.int32))
    emb_ln_g = 1.0 + nrm((D,), 0.02)
    emb_ln_b = nrm((D,), 0.02)
    ada_w = nrm((L, D, 6 * D), 0.1 * fan)
    ada_b = nrm((L, 6 * D), 0.02)
    w_in = jnp.concatenate([
        nrm((L, D, MLA_IN), fan),
        nrm((L, D, 2 * C), fan),
        nrm((L, D, C), fan * DEEPNORM_BETA),
        nrm((L, D, DECAY_LORA + ICLR_LORA + GATE_LORA), fan)], axis=-1)
    q_norm_g = 1.0 + nrm((L, Q_LORA_RANK), 0.02)
    w_uq = nrm((L, Q_LORA_RANK, MLA_HEADS * QK_HEAD_DIM), Q_LORA_RANK ** -0.5)
    kv_norm_g = 1.0 + nrm((L, KV_LORA_RANK), 0.02)
    w_uk = nrm((L, KV_LORA_RANK, MLA_HEADS * QK_NOPE_DIM), KV_LORA_RANK ** -0.5)
    w_uv = nrm((L, KV_LORA_RANK, MLA_HEADS * V_HEAD_DIM), KV_LORA_RANK ** -0.5 * DEEPNORM_BETA)
    mla_out_g = 1.0 + nrm((L, MLA_OUT), 0.02)
    rwkv_mu = jax.random.uniform(next(keys), (L, RWKV_IN), jnp.float32)
    ramp = jnp.linspace(0.0, 1.0, C) ** 0.85
    rwkv_w0 = -6.5 + 5.0 * ramp[None, :] + nrm((L, C), 0.1)
    rwkv_w2 = nrm((L, DECAY_LORA, C), 0.1 * DECAY_LORA ** -0.5)
    rwkv_a0 = nrm((L, C), 0.1)
    rwkv_a2 = nrm((L, ICLR_LORA, C), 0.1 * ICLR_LORA ** -0.5)
    rwkv_g2 = nrm((L, GATE_LORA, C), GATE_LORA ** -0.5)
    rwkv_k_k = 0.85 + nrm((L, C), 0.02)
    rwkv_k_a = 1.0 + nrm((L, C), 0.02)
    rwkv_r_k = nrm((L, RWKV_HEADS, RWKV_HEAD_DIM), 0.1)
    rwkv_gn_g = 1.0 + nrm((L, C), 0.02)
    rwkv_gn_b = nrm((L, C), 0.02)
    vres_v0 = 1.0 + nrm((L - 1, C), 0.1)
    vres_v1 = nrm((L - 1, C, VRES_LORA), C ** -0.5)
    vres_v2 = nrm((L - 1, VRES_LORA, C), 0.1 * VRES_LORA ** -0.5)
    w_o = nrm((L, MIX_DIM, D), MIX_DIM ** -0.5 * DEEPNORM_BETA)
    ln1_g = 1.0 + nrm((L, D), 0.02)
    ln1_b = nrm((L, D), 0.02)
    router_w = nrm((L, D, E), fan)
    router_b = nrm((L, E), 0.01)
    exp_w1 = nrm((L, E, D, 2 * F), fan)
    exp_b1 = nrm((L, E, 2 * F), 0.02)
    exp_w2 = nrm((L, E, F, D), F ** -0.5 * DEEPNORM_BETA)
    exp_b2 = nrm((L, E, D), 0.02)
    ln2_g = 1.0 + nrm((L, D), 0.02)
    ln2_b = nrm((L, D), 0.02)
    return {'x': x, 'c': c, 'positions': positions, 'emb_ln_g': emb_ln_g, 'emb_ln_b': emb_ln_b,
            'ada_w': ada_w, 'ada_b': ada_b, 'w_in': w_in,
            'q_norm_g': q_norm_g, 'w_uq': w_uq, 'kv_norm_g': kv_norm_g, 'w_uk': w_uk, 'w_uv': w_uv,
            'mla_out_g': mla_out_g, 'rwkv_mu': rwkv_mu, 'rwkv_w0': rwkv_w0, 'rwkv_w2': rwkv_w2,
            'rwkv_a0': rwkv_a0, 'rwkv_a2': rwkv_a2, 'rwkv_g2': rwkv_g2, 'rwkv_k_k': rwkv_k_k,
            'rwkv_k_a': rwkv_k_a, 'rwkv_r_k': rwkv_r_k, 'rwkv_gn_g': rwkv_gn_g, 'rwkv_gn_b': rwkv_gn_b,
            'vres_v0': vres_v0, 'vres_v1': vres_v1, 'vres_v2': vres_v2, 'w_o': w_o,
            'ln1_g': ln1_g, 'ln1_b': ln1_b, 'router_w': router_w, 'router_b': router_b,
            'exp_w1': exp_w1, 'exp_b1': exp_b1, 'exp_w2': exp_w2, 'exp_b2': exp_b2,
            'ln2_g': ln2_g, 'ln2_b': ln2_b}

def first_block(x, c, positions, emb_ln_g, emb_ln_b, ada_w, ada_b, w_in,
              q_norm_g, w_uq, kv_norm_g, w_uk, w_uv, mla_out_g,
              rwkv_mu, rwkv_w0, rwkv_w2, rwkv_a0, rwkv_a2, rwkv_g2, rwkv_k_k, rwkv_k_a, rwkv_r_k,
              rwkv_gn_g, rwkv_gn_b, vres_v0, vres_v1, vres_v2, w_o, ln1_g, ln1_b,
              router_w, router_b, exp_w1, exp_b1, exp_w2, exp_b2, ln2_g, ln2_b):
    inv_freq = ROPE_THETA ** (-jnp.arange(0, QK_ROPE_DIM, 2, dtype=jnp.float32) / QK_ROPE_DIM)
    ang = positions.astype(jnp.float32)[..., None] * inv_freq
    cos, sin = jnp.cos(ang), jnp.sin(ang)
    c_act = jax.nn.silu(c)
    x = layer_norm(x, emb_ln_g, emb_ln_b)
    v_first = None
    for i in range(DEPTH):
        mod = c_act @ ada_w[i] + ada_b[i]
        sh1, sc1, gt1, sh2, sc2, gt2 = [m[:, None, :] for m in jnp.split(mod, 6, axis=-1)]
        h = x * (1.0 + sc1) + sh1
        p = h @ w_in[i]
        mla_o = mla_group(p[..., :MLA_IN], cos, sin, q_norm_g[i], w_uq[i], kv_norm_g[i],
                          w_uk[i], w_uv[i], mla_out_g[i])
        vres = None if i == 0 else (vres_v0[i - 1], vres_v1[i - 1], vres_v2[i - 1])
        rwkv_o, v_i = rwkv7_group(p[..., MLA_IN:], rwkv_mu[i], rwkv_w0[i], rwkv_w2[i], rwkv_a0[i],
                                  rwkv_a2[i], rwkv_g2[i], rwkv_k_k[i], rwkv_k_a[i], rwkv_r_k[i],
                                  rwkv_gn_g[i], rwkv_gn_b[i], v_first, vres)
        if i == 0:
            v_first = v_i
        mix = jnp.concatenate([mla_o, rwkv_o], axis=-1) @ w_o[i]
        x = layer_norm(DEEPNORM_ALPHA * x + (1.0 + gt1) * mix, ln1_g[i], ln1_b[i])
        h = x * (1.0 + sc2) + sh2
        ffn = moe_ffn(h, router_w[i], router_b[i], exp_w1[i], exp_b1[i], exp_w2[i], exp_b2[i])
        x = layer_norm(DEEPNORM_ALPHA * x + (1.0 + gt2) * ffn, ln2_g[i], ln2_b[i])
    return x


DEPTH_2 = 2

D_MIX = D_MODEL
HEAD_DIM = 64
FOX_WIDTH = D_MIX // 4
DIL_WIDTH = D_MIX // 4
HGRN_WIDTH = D_MIX // 2
FOX_HEADS = FOX_WIDTH // HEAD_DIM
DIL_HEADS = DIL_WIDTH // HEAD_DIM
HGRN_EXPAND = 128
HGRN_HEADS = HGRN_WIDTH // HGRN_EXPAND
HGRN_VDIM = HGRN_WIDTH // HGRN_HEADS
HGRN_FDIM = HGRN_HEADS * HGRN_EXPAND
HGRN_CHUNK = 64
DILATED_PATTERNS = ((128, 1), (512, 4), (2048, 16))
ROPE_DIM = HEAD_DIM // 4
ROPE_THETA_2 = 500000.0
D_FF = ((8 * D_MODEL // 3 + 127) // 128) * 128
EPS = 1e-6
NEG_BIG = -1e30
LB_FLOOR = 1e-30

SPLIT_SIZES = (FOX_WIDTH, FOX_WIDTH, FOX_WIDTH, FOX_HEADS,
               DIL_WIDTH, DIL_WIDTH, DIL_WIDTH,
               HGRN_FDIM, HGRN_FDIM, HGRN_WIDTH, HGRN_WIDTH)
N_IN_2 = sum(SPLIT_SIZES)
SPLIT_POINTS = tuple(int(s) for s in np.cumsum(SPLIT_SIZES)[:-1])


def _rmsnorm(x, g):
    xf = x.astype(jnp.float32)
    y = xf * lax.rsqrt(jnp.mean(xf * xf, axis=-1, keepdims=True) + EPS)
    return (y * g.astype(jnp.float32)).astype(x.dtype)

def _swiglu(h, wg, wu, wd):
    return (jax.nn.silu(h @ wg) * (h @ wu)) @ wd

def _partial_rope(t, positions):
    half = ROPE_DIM // 2
    freqs = ROPE_THETA_2 ** (-jnp.arange(0, ROPE_DIM, 2, dtype=jnp.float32) / ROPE_DIM)
    ang = positions.astype(jnp.float32)[:, :, None] * freqs
    cos = jnp.cos(ang)[:, :, None, :]
    sin = jnp.sin(ang)[:, :, None, :]
    tf = t.astype(jnp.float32)
    x1, x2, rest = tf[..., :half], tf[..., half:ROPE_DIM], tf[..., ROPE_DIM:]
    out = jnp.concatenate([x1 * cos - x2 * sin, x2 * cos + x1 * sin, rest], axis=-1)
    return out.astype(t.dtype)

def _fox_attention(q, k, v, c):
    B, H, T, dh = q.shape
    nb = T // Q_BLOCK
    scale = dh ** -0.5
    qb = q.reshape(B, H, nb, Q_BLOCK, dh).transpose(2, 0, 1, 3, 4)
    cb = c.reshape(B, H, nb, Q_BLOCK).transpose(2, 0, 1, 3)
    kpos = jnp.arange(T)

    def block(args):
        qi, ci, n = args
        s = jnp.einsum('bhqd,bhkd->bhqk', qi, k).astype(jnp.float32) * scale
        s = s + ci[..., None] - c[:, :, None, :]
        qpos = n * Q_BLOCK + jnp.arange(Q_BLOCK)
        mask = kpos[None, :] <= qpos[:, None]
        p = jax.nn.softmax(jnp.where(mask, s, NEG_BIG), axis=-1)
        return jnp.einsum('bhqk,bhkd->bhqd', p.astype(v.dtype), v)

    out = lax.map(block, (qb, cb, jnp.arange(nb)))
    return out.transpose(1, 2, 0, 3, 4).reshape(B, H, T, dh)

def _dilated_branch(q, k, v, window, dilation):
    B, H, T, dh = q.shape
    L = T // dilation
    w = window // dilation
    blk = min(w, L)
    nb = -(-L // blk)
    Lp = nb * blk
    scale = dh ** -0.5

    def to_blocks(t):
        t = t.reshape(B, H, L, dilation, dh).transpose(0, 1, 3, 2, 4)
        t = jnp.pad(t, ((0, 0), (0, 0), (0, 0), (0, Lp - L), (0, 0)))
        return t.reshape(B, H, dilation, nb, blk, dh)

    def with_prev(t):
        prev = jnp.pad(t, ((0, 0), (0, 0), (0, 0), (1, 0), (0, 0), (0, 0)))[:, :, :, :nb]
        return jnp.concatenate([prev, t], axis=4)

    qb = to_blocks(q)
    kc = with_prev(to_blocks(k))
    vc = with_prev(to_blocks(v))
    s = jnp.einsum('bhrnqd,bhrnkd->bhrnqk', qb, kc).astype(jnp.float32) * scale
    i = jnp.arange(blk)[:, None]
    j = jnp.arange(2 * blk)[None, :]
    rel = blk + i - j
    first = (jnp.arange(nb)[:, None, None] == 0) & (j < blk)[None]
    mask = ((rel >= 0) & (rel <= w))[None] & ~first
    s = jnp.where(mask, s, NEG_BIG)
    m = jnp.max(s, axis=-1, keepdims=True)
    p = jnp.exp(s - m)
    den = jnp.sum(p, axis=-1)
    o = jnp.einsum('bhrnqk,bhrnkd->bhrnqd', p, vc.astype(jnp.float32)) / den[..., None]
    lse = m[..., 0] + jnp.log(den)
    o = o.reshape(B, H, dilation, Lp, dh)[:, :, :, :L].transpose(0, 1, 3, 2, 4).reshape(B, H, T, dh)
    lse = lse.reshape(B, H, dilation, Lp)[..., :L].transpose(0, 1, 3, 2).reshape(B, H, T)
    return o, lse

def _dilated_attention(q, k, v):
    outs, lses = [], []
    for window, dilation in DILATED_PATTERNS:
        o, lse = _dilated_branch(q, k, v, window, dilation)
        outs.append(o)
        lses.append(lse)
    wts = jax.nn.softmax(jnp.stack(lses, 0), axis=0)
    return jnp.sum(wts[..., None] * jnp.stack(outs, 0), axis=0)

def _hgrn2(q_raw, f_raw, i_raw, g_raw, lb, norm_w):
    B, T, _ = q_raw.shape
    H, E, V, C = HGRN_HEADS, HGRN_EXPAND, HGRN_VDIM, HGRN_CHUNK
    nc = T // C
    lbf = jnp.clip(lb.astype(jnp.float32), 0.0, 1.0 - 1e-6)
    z = f_raw.astype(jnp.float32)
    log_f = jnp.logaddexp(jnp.log(jnp.maximum(lbf, LB_FLOOR)),
                          jnp.log1p(-lbf) + jax.nn.log_sigmoid(z))
    kk = (1.0 - lbf) * jax.nn.sigmoid(-z)
    qq = jax.nn.silu(q_raw.astype(jnp.float32))
    vv = i_raw.astype(jnp.float32)

    def chunks(t, d):
        return t.reshape(B, nc, C, H, d).transpose(1, 0, 3, 2, 4)

    causal = jnp.arange(C)[:, None] >= jnp.arange(C)[None, :]

    def step(S, inp):
        q, k, v, lf = inp
        b = jnp.cumsum(lf, axis=2)
        inter = jnp.einsum('bhte,bhev->bhtv', q * jnp.exp(b), S)
        diff = b[:, :, :, None, :] - b[:, :, None, :, :]
        D = jnp.exp(jnp.where(causal[None, None, :, :, None], diff, NEG_BIG))
        A = jnp.einsum('bhtse,bhse->bhts', q[:, :, :, None, :] * D, k)
        intra = jnp.einsum('bhts,bhsv->bhtv', A, v)
        b_last = b[:, :, -1, :]
        S_new = jnp.exp(b_last)[..., None] * S + jnp.einsum(
            'bhse,bhsv->bhev', k * jnp.exp(b_last[:, :, None, :] - b), v)
        return S_new, inter + intra

    S0 = jnp.zeros((B, H, E, V), jnp.float32)
    _, o = lax.scan(step, S0, (chunks(qq, E), chunks(kk, E), chunks(vv, V), chunks(log_f, E)))
    o = o.transpose(1, 0, 3, 2, 4).reshape(B, T, H, V)
    o = o * lax.rsqrt(jnp.mean(o * o, axis=-1, keepdims=True) + EPS)
    o = o.reshape(B, T, H * V) * norm_w.astype(jnp.float32)
    return o * jax.nn.sigmoid(g_raw.astype(jnp.float32))

def _mixing(h, positions, w_in, w_out, fox_b, lb, hgrn_norm):
    B, T, _ = h.shape
    proj = h @ w_in
    (fq, fk, fv, ff, dq, dk, dv, hq, hf, hi, hg) = jnp.split(proj, SPLIT_POINTS, axis=-1)

    def heads(t, n):
        return t.reshape(B, T, n, HEAD_DIM)

    log_fg = jax.nn.log_sigmoid((ff + fox_b).astype(jnp.float32))
    c = jnp.cumsum(log_fg, axis=1).transpose(0, 2, 1)
    tr = lambda t: t.transpose(0, 2, 1, 3)
    oa = _fox_attention(tr(heads(fq, FOX_HEADS)), tr(heads(fk, FOX_HEADS)),
                        tr(heads(fv, FOX_HEADS)), c)
    oa = oa.transpose(0, 2, 1, 3).reshape(B, T, FOX_WIDTH)

    qd = _partial_rope(heads(dq, DIL_HEADS), positions)
    kd = _partial_rope(heads(dk, DIL_HEADS), positions)
    ob = _dilated_attention(tr(qd), tr(kd), tr(heads(dv, DIL_HEADS)))
    ob = ob.transpose(0, 2, 1, 3).reshape(B, T, DIL_WIDTH)

    oc = _hgrn2(hq, hf, hi, hg, lb, hgrn_norm)

    o = jnp.concatenate([oa.astype(h.dtype), ob.astype(h.dtype), oc.astype(h.dtype)], axis=-1)
    return o @ w_out

def second_inputs(seed: int = 0) -> dict:
    key = jax.random.key(seed)
    ks = jax.random.split(key, 20)
    f32 = jnp.float32
    nrm = lambda k, shape, fan: jax.random.normal(k, shape, f32) * fan ** -0.5
    gain = lambda k, shape: 1.0 + 0.02 * jax.random.normal(k, shape, f32)
    x = jax.random.normal(ks[0], (BATCH, SEQ, D_MODEL), f32)
    positions = jnp.broadcast_to(jnp.arange(SEQ, dtype=jnp.int32)[None, :], (BATCH, SEQ))
    return {
        "x": x,
        "positions": positions,
        "ffn1_norm": gain(ks[1], (DEPTH_2, D_MODEL)),
        "ffn1_w_gate": nrm(ks[2], (DEPTH_2, D_MODEL, D_FF), D_MODEL),
        "ffn1_w_up": nrm(ks[3], (DEPTH_2, D_MODEL, D_FF), D_MODEL),
        "ffn1_w_down": nrm(ks[4], (DEPTH_2, D_FF, D_MODEL), D_FF),
        "mix_norm": gain(ks[5], (DEPTH_2, D_MODEL)),
        "w_in": nrm(ks[6], (DEPTH_2, D_MODEL, N_IN_2), D_MODEL),
        "fox_forget_bias": 2.0 + 0.5 * jax.random.normal(ks[7], (DEPTH_2, FOX_HEADS), f32),
        "hgrn_lower_bounds": 0.1 * jax.random.normal(ks[8], (DEPTH_2, HGRN_FDIM), f32),
        "hgrn_out_norm": gain(ks[9], (DEPTH_2, HGRN_WIDTH)),
        "w_out": nrm(ks[10], (DEPTH_2, D_MIX, D_MODEL), D_MIX),
        "ffn2_norm": gain(ks[11], (DEPTH_2, D_MODEL)),
        "ffn2_w_gate": nrm(ks[12], (DEPTH_2, D_MODEL, D_FF), D_MODEL),
        "ffn2_w_up": nrm(ks[13], (DEPTH_2, D_MODEL, D_FF), D_MODEL),
        "ffn2_w_down": nrm(ks[14], (DEPTH_2, D_FF, D_MODEL), D_FF),
        "final_norm": gain(ks[15], (D_MODEL,)),
    }

def second_block(x, positions, ffn1_norm, ffn1_w_gate, ffn1_w_up, ffn1_w_down, mix_norm, w_in,
              fox_forget_bias, hgrn_lower_bounds, hgrn_out_norm, w_out, ffn2_norm,
              ffn2_w_gate, ffn2_w_up, ffn2_w_down, final_norm):
    sm = jax.nn.softmax(hgrn_lower_bounds.astype(jnp.float32), axis=0)
    lbs = jnp.cumsum(sm, axis=0) - sm[0:1]
    for i in range(DEPTH_2):
        h = _rmsnorm(x, ffn1_norm[i])
        x = x + 0.5 * _swiglu(h, ffn1_w_gate[i], ffn1_w_up[i], ffn1_w_down[i])
        h = _rmsnorm(x, mix_norm[i])
        x = x + _mixing(h, positions, w_in[i], w_out[i], fox_forget_bias[i], lbs[i],
                        hgrn_out_norm[i])
        h = _rmsnorm(x, ffn2_norm[i])
        x = x + 0.5 * _swiglu(h, ffn2_w_gate[i], ffn2_w_up[i], ffn2_w_down[i])
    return _rmsnorm(x, final_norm)


def setup_inputs(seed=0):
    out = dict(first_inputs(seed))
    for name, value in second_inputs(seed + 1).items():
        if name != "x":
            out[name + "_2"] = value
    return out


def reference(
    x, c, positions, emb_ln_g, emb_ln_b, ada_w, ada_b, w_in, q_norm_g, w_uq, kv_norm_g, w_uk,
    w_uv, mla_out_g, rwkv_mu, rwkv_w0, rwkv_w2, rwkv_a0, rwkv_a2, rwkv_g2, rwkv_k_k, rwkv_k_a,
    rwkv_r_k, rwkv_gn_g, rwkv_gn_b, vres_v0, vres_v1, vres_v2, w_o, ln1_g, ln1_b, router_w,
    router_b, exp_w1, exp_b1, exp_w2, exp_b2, ln2_g, ln2_b, positions_2, ffn1_norm_2,
    ffn1_w_gate_2, ffn1_w_up_2, ffn1_w_down_2, mix_norm_2, w_in_2, fox_forget_bias_2,
    hgrn_lower_bounds_2, hgrn_out_norm_2, w_out_2, ffn2_norm_2, ffn2_w_gate_2, ffn2_w_up_2,
    ffn2_w_down_2, final_norm_2,
):
    x = first_block(
        x, c, positions, emb_ln_g, emb_ln_b, ada_w, ada_b, w_in, q_norm_g, w_uq, kv_norm_g,
        w_uk, w_uv, mla_out_g, rwkv_mu, rwkv_w0, rwkv_w2, rwkv_a0, rwkv_a2, rwkv_g2, rwkv_k_k,
        rwkv_k_a, rwkv_r_k, rwkv_gn_g, rwkv_gn_b, vres_v0, vres_v1, vres_v2, w_o, ln1_g, ln1_b,
        router_w, router_b, exp_w1, exp_b1, exp_w2, exp_b2, ln2_g, ln2_b,
    )
    return second_block(
        x, positions_2, ffn1_norm_2, ffn1_w_gate_2, ffn1_w_up_2, ffn1_w_down_2, mix_norm_2,
        w_in_2, fox_forget_bias_2, hgrn_lower_bounds_2, hgrn_out_norm_2, w_out_2, ffn2_norm_2,
        ffn2_w_gate_2, ffn2_w_up_2, ffn2_w_down_2, final_norm_2,
    )


_drawn_inputs = setup_inputs


def setup_inputs(seed=0):
    import zlib

    import numpy as np

    out = dict(_drawn_inputs(seed))
    spreads = {}
    factors = {'q_norm_g': 3.226,
     'kv_norm_g': 3.079,
     'mla_out_g': 2.913,
     'rwkv_w2': 4.918,
     'rwkv_a2': 3.145,
     'rwkv_k_k': 5.948,
     'rwkv_k_a': 5.257,
     'rwkv_gn_g': 4.098,
     'rwkv_gn_b': 4.517,
     'router_b': 3.451,
     'exp_b1': 7.83,
     'exp_b2': 5.177,
     'ffn1_norm_2': 4.718,
     'mix_norm_2': 4.033,
     'hgrn_lower_bounds_2': 32.443,
     'hgrn_out_norm_2': 24.764,
     'ffn2_norm_2': 5.658,
     'final_norm_2': 8.212}
    for name, (base, spread) in spreads.items():
        noise = np.random.default_rng([zlib.crc32(name.encode()), seed]).standard_normal(out[name].shape)
        drawn = base * np.exp(spread * noise) if base else spread * noise
        out[name] = jnp.asarray(drawn.astype(out[name].dtype))
    for name, factor in factors.items():
        out[name] = (out[name] * factor).astype(out[name].dtype)
    return out
```

```python
from contextlib import ExitStack

import numpy as np

import concourse.bass as bass
from concourse import mybir

ALU = mybir.AluOpType
ACT = mybir.ActivationFunctionType
F32 = mybir.dt.float32
F32R = mybir.dt.float32r
I32 = mybir.dt.int32
U8 = mybir.dt.uint8
AX_X = mybir.AxisListType.X

P = 128
T = 256
TT = T // P
D = 1024
DC = D // P
ALPHA = 2.0 ** 0.25

HEADS = 8
NOPE, ROPE, VDIM = 64, 32, 64
QLORA, KVLORA = 256, 128
RW = 512
HP = RW // P
RWT = 14
CH = 64
NCH = T // CH
EXP_M05 = float(np.exp(-0.5))
E = 32
TOPK = 4
F_E = 1024
SLOTS = 64
LIMIT, SW_ALPHA = 7.0, 1.702

LAYERS = 2
D_FF = 2816
FT = D_FF // P
LB_FLOOR = 1e-30

RING = 12
SLOT = 2048
ADA_UNITS, IN_UNITS, WO_UNITS = 24, 8, 4
EXPERT_UNITS = 12
FFN_UNITS, MIX_UNITS, WOUT_UNITS = 33, 14, 4
LAYER_UNITS = 2 * FFN_UNITS + MIX_UNITS + WOUT_UNITS
U_ADA = 0
U_IN = U_ADA + ADA_UNITS
U_WO = U_IN + IN_UNITS
U_EXP = U_WO + WO_UNITS
U_LAYER = U_EXP + E * EXPERT_UNITS
assert LAYER_UNITS % RING == 0 and U_EXP % RING == 0 and EXPERT_UNITS == RING

TWO_PI = 2 * np.pi
PI_1 = 6.28125
PI_2 = float(np.float32(np.round((TWO_PI - PI_1) * 2.0 ** 20) / 2.0 ** 20))
PI_3 = float(np.float32(TWO_PI - PI_1 - PI_2))
ROUND = 1.5 * 2.0 ** 23
NEG = -1.0e30


def shape_constants():
    i = np.arange(P)
    f = np.float32
    base, rwkv = {}, {}
    base["ident"] = np.eye(P)
    base["ones"] = np.ones((P, P))
    base["heads64"] = (i[:, None] // 64 == i[None] // 64)
    r = np.zeros((P, P))
    for h in range(0, P, 64):
        for d in range(8):
            r[h + d + 8, h + d] = -1
            r[h + d, h + d + 8] = 1
    base["rot_dil"] = r
    r = np.zeros((P, ROPE))
    for d in range(0, ROPE, 2):
        r[d + 1, d] = -1
        r[d, d + 1] = 1
    base["rot_mla"] = r
    q = i[:, None, None] + P * np.arange(TT)[None, :, None]
    k = np.arange(T)[None, None, :]
    base["causal"] = np.where(k <= q, 0.0, NEG).reshape(P, -1)
    gap = q - k
    count = (gap <= 128).astype(int) + (gap % 4 == 0) + (gap % 16 == 0)
    count = np.where(gap >= 0, count, 0)
    base["dilated"] = np.where(count > 0, 8.0 * np.log(np.maximum(count, 1)), NEG).reshape(P, -1)
    sel = np.zeros((P, 4, P))
    for h in range(4):
        sel[h, h] = 1
    base["pick_head"] = sel.reshape(P, -1)
    base["before"] = (i[:, None] < i[None])
    base["slot"] = np.tile(np.arange(SLOTS), (P, 1))
    base["rev"] = np.tile(E - np.arange(E), (P, 1))
    inv = (np.float32(10000.0) ** (-np.arange(0, ROPE, 2, dtype=f) / f(ROPE))).astype(f)
    col = np.zeros((P, 1))
    col[:ROPE, 0] = np.repeat(inv, 2)
    base["freq_mla"] = col
    inv = (np.float32(500000.0) ** (-np.arange(0, 16, 2, dtype=f) / f(16))).astype(f)
    col = np.zeros((P, 1))
    for h in range(0, P, 64):
        col[h:h + 8, 0] = inv
        col[h + 8:h + 16, 0] = inv
    base["freq_dil"] = col
    same = i[:, None] // CH == i[None] // CH
    rwkv["above"] = same & (i[:, None] < i[None])
    rwkv["below"] = same & (i[:, None] > i[None])
    rwkv["above_eq"] = same & (i[:, None] <= i[None])
    for b in (1, 2, 4, 8, 16, 32):
        m = (i[:, None] // (2 * b) == i[None] // (2 * b)) & (i[:, None] % (2 * b) >= b) & (i[None] % (2 * b) < b)
        rwkv[f"lower{b}"] = m
        if b == 1:
            rwkv["lower1_t"] = m.T
    rwkv["no_start"] = np.tile((np.arange(HP * T) % CH != 0), (P, 1))
    levels = [i[:, None] == i[None]]
    for b in (1, 2, 4, 8, 16, 32, 64):
        levels.append((i[:, None] // (2 * b) == i[None] // (2 * b)) & (i[None] % (2 * b) >= b) & (i[:, None] % (2 * b) < b))
    return base, rwkv, np.concatenate(levels, 1).astype(np.float32)


def columns(parts):
    at, where = 0, {}
    for name, a in parts.items():
        where[name] = (at, a.shape[1])
        at += a.shape[1]
    return where, at


BASE_PARTS, RWKV_PARTS, LEVEL_MASKS = shape_constants()
BASE_AT, BASE_N = columns(BASE_PARTS)
RWKV_AT, RWKV_N = columns(RWKV_PARTS)
NLEV = 8

ROWS_A = [("emb_ln_g", 8), ("emb_ln_b", 8), ("ada_b", 48), ("q_norm_g", 2), ("kv_norm_g", 1), ("mla_out_g", 4),
          ("rwkv_mu", 14), ("rwkv_w0", 4), ("rwkv_a0", 4), ("rwkv_k_k", 4), ("rwkv_k_a", 4), ("rwkv_r_k", 4),
          ("rwkv_gn_g", 4), ("rwkv_gn_b", 4), ("ln1_g", 8)]
ROWS_B = [("ln1_b", 8), ("c", 8), ("ln2_g", 8), ("ln2_b", 8), ("ffn1_norm_2", 16), ("mix_norm_2", 16),
          ("hgrn_lower_bounds_2", 8), ("hgrn_out_norm_2", 8), ("ffn2_norm_2", 16), ("final_norm_2", 8)]


def row_places(rows, base):
    at, out = base, {}
    for name, n in rows:
        out[name] = at
        at += n
    assert at - base <= P
    return out, at - base


AT_A, N_A = row_places(ROWS_A, 0)
AT_B, N_B = row_places(ROWS_B, P)
AT = {**AT_A, **AT_B}


class Steps:

    def __init__(self, engine, sem, own):
        self.engine, self.sem, self.own, self.count = engine, sem, own, {}

    def tell(self, ins, name):
        self.count[name] = self.count.get(name, 0) + 1
        ins.then_inc(self.sem(name), 1)

    def step(self, ins, name=None):
        name = name or self.own
        self.tell(ins, name)
        self.engine.wait_ge(self.sem(name), self.count[name])


class Stage:

    POOL = 48

    def __init__(self, nc, pool):
        self.nc, self.pool = nc, pool

    def __enter__(self):
        self.names = {}
        self.block = self.nc.Block()
        self.block.__enter__()
        return self

    def sem(self, name):
        return self.pool[self.names.setdefault(name, len(self.names))]

    def __exit__(self, *e):
        self.block.__exit__(*e)
        if e[0] is None and self.names:
            first = self.pool[0].num
            assert [s.num for s in self.pool] == list(range(first, first + len(self.pool)))
            self.nc.all_engine_barrier(sems_to_clear=range(first, first + len(self.names)))
        return False


def build(nc, A, out, stop=None):
    with ExitStack() as ctx:
        names = {}

        def sb(name, shape, dt=F32, where=ctx):
            names[name] = names.get(name, 0) + 1
            if names[name] > 1:
                name = f"{name}_{names[name]}"
            return where.enter_context(nc.sbuf_tensor(name, shape, dt))

        ring = sb("ring", [P, RING, SLOT])
        xT = sb("xT", [P, DC, T])
        hT = sb("hT", [P, DC, T])
        base = sb("base", [P, BASE_N])
        params = sb("params", [P, 2 * P])
        mod = sb("mod", [P, 48])
        bank = [ctx.enter_context(nc.psum_tensor(f"bank{i}", [P, 512], F32)) for i in range(8)]
        loaded = [ctx.enter_context(nc.semaphore(f"slot_loaded{i}")) for i in range(RING)]
        pool = [ctx.enter_context(nc.semaphore(f"stage{i}")) for i in range(Stage.POOL)]
        loaded2 = [ctx.enter_context(nc.semaphore(f"slot_loaded_2_{i}")) for i in range(RING)]
        used2 = ctx.enter_context(nc.semaphore("ring_units_used_2"))
        assert used2.num - loaded2[0].num == RING
        used = ctx.enter_context(nc.semaphore("ring_units_used"))

        def const(name):
            at, n = BASE_AT[name]
            return base[:, at:at + n]

        ident, ones, heads64 = const("ident"), const("ones"), const("heads64")

        def par(name, c=0, n=1):
            return params[:, AT[name] + c:AT[name] + c + n]

        def slot3(u, c):
            return ring[:, u % RING, :].rearrange("p (c n) -> p c n", c=c)

        def load_unit(sp, u, dst, src, shift=0):
            if u >= RING or not isinstance(shift, int):
                sp.wait_ge(used, shift + (u - RING + 1))
            sp.dma_start(dst, src).then_inc(loaded[u % RING], 16)

        def unit_ready(pe, u, rounds=0):
            pe.wait_ge(loaded[u % RING], 16 * (u // RING + 1) + 16 * rounds if isinstance(rounds, int)
                       else rounds * 16 + 16 * (u // RING + 1))

        def cols8(w, c0, n=256):
            return w[:, c0:c0 + n].rearrange("(c p) n -> p c n", p=P)

        block1 = ctx.enter_context(ExitStack())
        ps = sb("ps", [P, RWT, T], where=block1)
        mla = block1.enter_context(ExitStack())
        q_lat = sb("q_lat", [P, 2, T], where=mla)
        kv_lat = sb("kv_lat", [P, T], where=mla)
        k_rot = sb("k_rot", [ROPE, T], where=mla)
        w_kv = sb("w_kv", [P, DC, KVLORA + ROPE], where=mla)
        w_uq = sb("w_uq", [P, 2, HEADS * (NOPE + ROPE)], where=mla)
        w_uk = sb("w_uk", [P, HEADS * NOPE], where=mla)
        w_uv = sb("w_uv", [P, HEADS * VDIM], where=mla)
        posi = sb("posi", [ROPE, T], I32, where=mla)
        small = ctx.enter_context(nc.semaphore("small_weights_loaded"))

        with ExitStack() as c1, Stage(nc, pool) as S:
            x_in = sb("x_in", [P, TT, D], where=c1)
            rows = sb("param_rows", [P, 2, P], where=c1)
            stats = sb("stats", [P, TT, 2, 6], where=c1)
            mv = sb("mv", [P, TT, 2], where=c1)
            rstd = sb("rstd", [P, TT], where=c1)
            c_act = sb("c_act", [P, 8], where=c1)
            sem = S.sem

            @S.block.sync
            def _(sp):
                sp.dma_start(x_in[:, :, :], A["x"][0].rearrange("(a p) d -> p a d", p=P)).then_inc(sem("x_loaded"), 16)
                sp.dma_start(base[:, :], A["const_base"]).then_inc(sem("base_loaded"), 16)
                sp.wait_ge(sem("rows_loaded"), 16 * (len(ROWS_A) + len(ROWS_B)))
                sp.wait_ge(sem("base_loaded"), 16)
                for u in range(ADA_UNITS):
                    load_unit(sp, u, slot3(u, DC), cols8(A["ada_w"][0], 256 * u))
                for n, u in enumerate(range(U_IN, U_IN + IN_UNITS)):
                    at = 0 if n == 0 else 416 + 256 * (n - 1)
                    load_unit(sp, u, slot3(u, DC), cols8(A["w_in"][0], at))

            @S.block.scalar
            def _(act):
                st = Steps(act, sem, "act_step")
                act.sem_inc(sem("mod_taken"), 2)
                for tile, table in ((0, ROWS_A), (1, ROWS_B)):
                    at = 0
                    for name, n in table:
                        act.dma_start(rows[at:at + n, tile, :], flat_rows(A[name])).then_inc(sem("rows_loaded"), 16)
                        at += n
                act.dma_start(w_kv[:, :, :], cols8(A["w_in"][0], QLORA, KVLORA + ROPE)).then_inc(small, 16)
                act.dma_start(w_uq[:, :, :], A["w_uq"][0].rearrange("(c p) n -> p c n", p=P)).then_inc(small, 16)
                act.dma_start(w_uk[:, :], A["w_uk"][0]).then_inc(small, 16)
                act.dma_start(w_uv[:, :], A["w_uv"][0]).then_inc(small, 16)
                act.dma_start(posi[:, :], A["positions"].to_broadcast([ROPE, T])).then_inc(small, 16)
                act.wait_ge(sem("mv_ready"), 2)
                st.tell(nc.scalar.activation(rstd[:, :], mv[:, :, 1], ACT.Sqrt, bias=1e-5), "root_ready")
                act.wait_ge(sem("params_ready"), 2)
                st.tell(nc.scalar.activation(c_act[:, :], par("c", 0, 8), ACT.Silu), "c_ready")
                with act.Fori(0, ADA_UNITS // RING) as i:
                    for k in range(RING // 2):
                        act.wait_ge(used, i * RING + (2 * k + 2))
                        tiles = bank[2 + k % 2][:, :].rearrange("p (m n) -> p m n", n=P)
                        nc.scalar.activation(mod[:, bass.ds(i * (2 * RING) + 4 * k, 4)], tiles[:, :, 0], ACT.Copy).then_inc(sem("mod_taken"), 1)

            @S.block.vector
            def _(dve):
                st = Steps(dve, sem, "dve_step")
                dve.wait_ge(sem("x_loaded"), 16)
                for a in range(TT):
                    nc.vector.bn_stats(stats[:, a, 0, :], x_in[:, a, 0:512])
                    st.step(nc.vector.bn_stats(stats[:, a, 1, :], x_in[:, a, 512:1024]))
                    st.tell(nc.vector.bn_aggr(mv[:, a, :], stats[:, a, :, :].rearrange("p a b -> p (a b)")), "mv_ready")
                dve.wait_ge(sem("root_ready"), 1)
                st.step(nc.vector.reciprocal(rstd[:, :], rstd[:, :]))
                for a in range(TT):
                    st.tell(nc.vector.tensor_scalar(x_in[:, a, :], x_in[:, a, :], mv[:, a, 0:1], rstd[:, a:a + 1],
                                                    ALU.subtract, ALU.mult), "x_normed")
                dve.wait_ge(sem("params_turned"), 2)
                st.tell(nc.vector.tensor_copy(params[:, 0:N_A], bank[0][:, 0:N_A]), "params_ready")
                st.step(nc.vector.tensor_copy(params[:, P:P + N_B], bank[1][:, 0:N_B]), "params_ready")
                for c in range(DC):
                    dve.wait_ge(sem("x_turned"), c + 1)
                    st.tell(nc.vector.tensor_scalar(xT[:, c, :], bank[4 + c % 4][:, 0:T], par("emb_ln_g", c), par("emb_ln_b", c),
                                                    ALU.mult, ALU.add), "xT_ready")
                dve.wait_ge(sem("mod_taken"), 2 + ADA_UNITS // 2)
                st.step(nc.vector.tensor_tensor(mod[:, :], mod[:, :], par("ada_b", 0, 48), ALU.add))
                st.step(nc.vector.tensor_scalar(mod[:, 8:16], mod[:, 8:16], 1.0, None, ALU.add))
                st.step(nc.vector.tensor_scalar(mod[:, 32:40], mod[:, 32:40], 1.0, None, ALU.add))
                st.step(nc.vector.tensor_scalar(mod[:, 16:24], mod[:, 16:24], 1.0, None, ALU.add))
                st.step(nc.vector.tensor_scalar(mod[:, 40:48], mod[:, 40:48], 1.0, None, ALU.add))
                for c in range(DC):
                    nc.vector.tensor_scalar(hT[:, c, :], xT[:, c, :], mod[:, 8 + c:9 + c], mod[:, c:c + 1], ALU.mult, ALU.add)

            @S.block.tensor
            def _(pe):
                pe.wait_ge(sem("base_loaded"), 16)
                pe.wait_ge(sem("rows_loaded"), 16 * (len(ROWS_A) + len(ROWS_B)))
                nc.tensor.transpose(bank[0][:, 0:N_A], rows[0:N_A, 0, :], ident[0:N_A, 0:N_A]).then_inc(sem("params_turned"), 1)
                nc.tensor.transpose(bank[1][:, 0:N_B], rows[0:N_B, 1, :], ident[0:N_B, 0:N_B]).then_inc(sem("params_turned"), 1)
                pe.wait_ge(sem("x_normed"), TT)
                for c in range(DC):
                    if c >= 4:
                        pe.wait_ge(sem("xT_ready"), c - 3)
                    for a in range(TT):
                        ins = nc.tensor.transpose(bank[4 + c % 4][:, P * a:P * a + P], x_in[:, a, P * c:P * c + P], ident)
                    ins.then_inc(sem("x_turned"), 1)
                pe.wait_ge(sem("c_ready"), 1)
                with pe.Fori(0, ADA_UNITS // RING) as i:
                    for u in range(RING):
                        unit_ready(pe, u, i)
                        w = slot3(u, DC)
                        if u % 2 == 0:
                            pe.wait_ge(sem("mod_taken"), i * (RING // 2) + (u // 2 + 1))
                        for j in range(2):
                            at = P * (2 * (u % 2) + j)
                            for c in range(DC):
                                ins = nc.tensor.matmul(bank[2 + u // 2 % 2][:, at:at + P], w[:, c, P * j:P * j + P],
                                                       c_act[:, c:c + 1].to_broadcast([P, P]), start=(c == 0), stop=(c == DC - 1))
                        ins.then_inc(used, 1)
        if stop == "embed":
            return

        def parts_of(high, rest):
            return ((high[0], rest[0]), (high[1], rest[0]), (high[0], rest[1]))

        with ExitStack() as c2, Stage(nc, pool) as S:
            raw = sb("raw", [P, 2, T + 1], where=c2)
            diff = sb("diff", [P, 2, T], where=c2)
            sem = S.sem
            N_MLA = 4
            h_parts = [sb(f"h_{part}", [P, DC, T], F32R, where=c2) for part in ("high", "low")]
            w_parts = [sb(f"w_{part}", [P, 3, DC, P], F32R, where=c2) for part in ("high", "low")]
            N_SPLIT = N_MLA - 2 + RWT

            def tile_weights(s_):
                return slot3(U_IN + s_ // 2, DC)[:, :, P * (s_ % 2):P * (s_ % 2) + P]

            def tile_low(dve, s_):
                dve.wait_ge(sem("high_ready"), s_ + 1)
                nc.vector.tensor_tensor(w_parts[1][:, s_ % 3, :, :], tile_weights(s_), w_parts[0][:, s_ % 3, :, :].bitcast(F32),
                                        ALU.subtract).then_inc(sem("low_ready"), 1)

            def tile_high(act, s_):
                act.wait_ge(loaded[(U_IN + s_ // 2) % RING], 16 * ((U_IN + s_ // 2) // RING + 1))
                if s_ >= 3:
                    act.wait_ge(sem("tile_ready"), s_)
                nc.scalar.activation(w_parts[0][:, s_ % 3, :, :], tile_weights(s_), ACT.Copy).then_inc(sem("high_ready"), 1)

            @S.block.sync
            def _(sp):
                pass

            @S.block.tensor
            def _(pe):
                pe.wait_ge(small, 16 * 5)
                for n, (at, m) in enumerate(((0, P), (P, ROPE))):
                    for c in range(DC):
                        ins = nc.tensor.matmul(bank[n][0:m, 0:T], w_kv[:, c, at:at + m], hT[:, c, :], start=(c == 0), stop=(c == DC - 1))
                    ins.then_inc(sem("tile_ready"), 1)
                pe.wait_ge(sem("h_low_ready"), 2)
                for n in range(2, N_MLA + RWT):
                    pe.wait_ge(sem("low_ready"), n - 1)
                    if n >= 8:
                        pe.wait_ge(sem("tile_taken"), n - 7)
                    for k, (w, h) in enumerate(parts_of([part[:, (n - 2) % 3, :, :] for part in w_parts], h_parts)):
                        for c in range(DC):
                            ins = nc.tensor.matmul(bank[n % 8][:, 0:T], w[:, c, :], h[:, c, :], start=(k == 0 and c == 0), stop=(k == 2 and c == DC - 1))
                            if k == 0 and c == 0 and n >= 4 and n % 2 == 0:
                                ins.then_inc(used, 1)
                    ins.then_inc(sem("tile_ready"), 1)
                pe.wait_ge(sem("tile_ready"), N_MLA + RWT)
                pe.sem_inc(used, 1)
            @S.block.scalar
            def _(act):
                for j in range(2):
                    four = slice(4 * j, 4 * j + 4)
                    nc.scalar.activation(h_parts[0][:, four, :], hT[:, four, :], ACT.Copy).then_inc(sem("h_high_ready"), 1)
                for s_ in range(3):
                    tile_high(act, s_)
                for n, dst in enumerate((kv_lat[:, :], k_rot[:, :], q_lat[:, 0, :], q_lat[:, 1, :])):
                    act.wait_ge(sem("tile_ready"), n + 1)
                    nc.scalar.activation(dst, bank[n][0:dst.shape[0], 0:T], ACT.Copy).then_inc(sem("tile_taken"), 1)
                act.wait_ge(sem("raw_cleared"), 1)
                for n in range(RWT):
                    if n + 3 < N_SPLIT:
                        tile_high(act, n + 3)
                    act.wait_ge(sem("tile_ready"), N_MLA + n + 1)
                    if n >= 2:
                        act.wait_ge(sem("shifted"), n - 1)
                    nc.scalar.activation(raw[:, n % 2, 1:T + 1], bank[(N_MLA + n) % 8][:, 0:T], ACT.Copy).then_inc(sem("raw_ready"), 1)

            @S.block.vector
            def _(dve):
                st = Steps(dve, sem, "dve_step")
                st.tell(nc.vector.memset(raw[:, :, 0:1], 0.0), "raw_cleared")
                dve.wait_ge(sem("raw_cleared"), 1)
                for j in range(2):
                    four = slice(4 * j, 4 * j + 4)
                    dve.wait_ge(sem("h_high_ready"), j + 1)
                    nc.vector.tensor_tensor(h_parts[1][:, four, :], hT[:, four, :], h_parts[0][:, four, :].bitcast(F32),
                                            ALU.subtract).then_inc(sem("h_low_ready"), 1)
                for s_ in range(3):
                    tile_low(dve, s_)
                for n in range(RWT):
                    if n + 3 < N_SPLIT:
                        tile_low(dve, n + 3)
                    dve.wait_ge(sem("raw_ready"), n + 1)
                    p_now = bank[(N_MLA + n) % 8][:, 0:T]
                    st.step(nc.vector.tensor_tensor(diff[:, n % 2, :], raw[:, n % 2, 0:T], p_now, ALU.subtract), "shifted")
                    st.tell(nc.vector.scalar_tensor_tensor(ps[:, n, :], diff[:, n % 2, :], par("rwkv_mu", n), p_now,
                                                           ALU.mult, ALU.add), "tile_taken")
        if stop == "inproj":
            return


        def attention(n, scale):

            def turn(pe, sem, S, i):
                pe.wait_ge(sem("probs_scaled"), i + 1)
                if i >= 2:
                    pe.wait_ge(sem("turned_taken"), i - 1)
                b = bank[2 + i % 2]
                nc.tensor.transpose(b[:, 0:P], S.probs[:, i % 2, 0, 0:P], ident)
                nc.tensor.transpose(b[:, P:2 * P], S.probs[:, i % 2, 1, 0:P], ident)
                nc.tensor.transpose(b[:, 2 * P:3 * P], S.probs[:, i % 2, 1, P:T], ident).then_inc(sem("probs_turned"), 1)

            def values(pe, sem, S, i, v):
                pe.wait_ge(sem("turned_taken"), i + 1)
                if i >= 4 and i % 2 == 0:
                    pe.wait_ge(sem("out_taken"), i // 2 - 1)
                o = bank[4 + i // 2 % 2][64 * (i % 2):64 * (i % 2) + 64, :]
                nc.tensor.matmul(o[:, 0:T], v(0), S.turned[:, i % 2, 0:T], start=True, stop=False, skip_group_check=True)
                nc.tensor.matmul(o[:, P:T], v(1), S.turned[:, i % 2, T:T + P], start=False, stop=True,
                                 skip_group_check=True).then_inc(sem("out_ready"), 1)

            def tensor(pe, S, scores, v, between=lambda i: None):
                sem = S.sem
                for i in range(n + 2):
                    if i < n:
                        if i >= 2:
                            pe.wait_ge(sem("masked"), i - 1)
                        for a in range(TT):
                            parts = scores(i, a)
                            for j, (lhs, rhs) in enumerate(parts):
                                ins = nc.tensor.matmul(bank[i % 2][:, T * a:T * a + T], lhs, rhs, start=(j == 0), stop=(j == len(parts) - 1))
                        ins.then_inc(sem("scores_ready"), 1)
                    between(i)
                    if 1 <= i <= n:
                        turn(pe, sem, S, i - 1)
                    if i >= 2:
                        values(pe, sem, S, i - 2, lambda a, h=i - 2: v(h, a))

            def vector(dve, st, S, mask, dst, between=lambda i: None):
                sem = S.sem
                for i in range(n + 3):
                    if i < n:
                        b = i % 2
                        dve.wait_ge(sem("scores_ready"), i + 1)
                        if i >= 2:
                            dve.wait_ge(sem("probs_ready"), 2 * (i - 1))
                        st.step(nc.vector.tensor_tensor(S.masked[:, b, :, :], bank[i % 2][:, :].rearrange("p (a k) -> p a k", a=TT),
                                                        mask(i), ALU.add), "masked")
                        st.step(nc.vector.tensor_reduce(S.peak[:, b, :], S.masked[:, b, :, :], AX_X, ALU.max))
                        st.tell(nc.vector.tensor_scalar(S.shift[:, b, :], S.peak[:, b, :], -scale, None, ALU.mult), "peak_ready")
                    if 1 <= i <= n:
                        b = (i - 1) % 2
                        dve.wait_ge(sem("probs_ready"), 2 * i)
                        st.step(nc.vector.reciprocal(S.den[:, b, :], S.den[:, b, :]))
                        nc.vector.tensor_scalar(S.probs[:, b, 0, 0:P], S.probs[:, b, 0, 0:P], S.den[:, b, 0:1], None, ALU.mult)
                        st.tell(nc.vector.tensor_scalar(S.probs[:, b, 1, :], S.probs[:, b, 1, :], S.den[:, b, 1:2], None, ALU.mult),
                                "probs_scaled")
                    if i >= 3 and (i - 3) % 2 == 1:
                        pair = (i - 3) // 2
                        dve.wait_ge(sem("out_ready"), i - 2)
                        st.tell(nc.vector.tensor_copy(dst(pair), bank[4 + pair % 2][:, 0:T]), "out_taken")
                    between(i)

            def scalar(act, st, S):
                sem = S.sem
                for i in range(n + 1):
                    if i < n:
                        b = i % 2
                        act.wait_ge(sem("peak_ready"), i + 1)
                        if i >= 2:
                            act.wait_ge(sem("probs_turned"), i - 1)
                        for a in range(TT):
                            st.tell(nc.scalar.activation(S.probs[:, b, a, :], S.masked[:, b, a, :], ACT.Exp, bias=S.shift[:, b, a:a + 1],
                                                         scale=scale, accum_out=S.den[:, b, a:a + 1]), "probs_ready")
                    if i >= 1:
                        b = (i - 1) % 2
                        act.wait_ge(sem("probs_turned"), i)
                        if i >= 3:
                            act.wait_ge(sem("out_ready"), i - 2)
                        st.tell(nc.scalar.activation(S.turned[:, b, :], bank[2 + b][:, 0:3 * P], ACT.Copy), "turned_taken")

            return tensor, vector, scalar

        def attention_buffers(S, where):
            S.masked = sb("masked", [P, 2, TT, T], where=where)
            S.probs = sb("probs", [P, 2, TT, T], where=where)
            S.turned = sb("turned", [P, 2, 3 * P], where=where)
            S.peak = sb("peak", [P, 2, TT], where=where)
            S.shift = sb("shift", [P, 2, TT], where=where)
            S.den = sb("den", [P, 2, TT], where=where)

        def rope_tables(dve, st, pos, freq, ang, turns, cos, sin):
            st.step(nc.vector.tensor_scalar(ang, pos, freq, None, ALU.mult))
            st.step(nc.vector.tensor_scalar(turns, ang, 1.0 / TWO_PI, ROUND, ALU.mult, ALU.add))
            st.step(nc.vector.tensor_scalar(turns, turns, ROUND, None, ALU.subtract))
            for part in (PI_1, PI_2, PI_3):
                st.step(nc.vector.scalar_tensor_tensor(ang, turns, -part, ang, ALU.mult, ALU.add))
            st.step(nc.vector.tensor_scalar(sin, ang, 3.1415925, -3.1415925, ALU.min, ALU.max))
            st.step(nc.vector.scalar_tensor_tensor(cos, sin, -1.0, sin, ALU.mult, ALU.min))
            st.tell(nc.vector.tensor_scalar(cos, cos, np.pi / 2, None, ALU.add), "angles_ready")

        with ExitStack() as c3, Stage(nc, pool) as S:
            sem = S.sem
            sq = sb("sq", [P, 4, T], where=c3)
            root = sb("root", [P, 2, T], where=c3)
            q_nope, k_nope, q_rope, tmp = (ring[0:n, U_WO % RING + j, :].rearrange("p (h t) -> p h t", t=T)
                                           for j, n in enumerate((NOPE, NOPE, ROPE, ROPE)))
            v_nat = sb("v_nat", [P, TT, HEADS * VDIM], where=c3)
            tab = sb("tab", [ROPE, 4, T], where=c3)
            posf = sb("posf", [ROPE, T], where=c3)
            attention_buffers(S, c3)
            causal = const("causal").rearrange("p (a k) -> p a k", a=TT)
            att_pe, att_dve, att_act = attention(HEADS, float((NOPE + ROPE) ** -0.5))

            @S.block.tensor
            def _(pe):
                pe.wait_ge(sem("squares"), 2)
                for c in range(2):
                    nc.tensor.matmul(bank[6][:, 0:T], ones, sq[:, c, :], start=(c == 0), stop=(c == 1))
                nc.tensor.matmul(bank[7][:, 0:T], ones, sq[:, 2, :], start=True, stop=True).then_inc(sem("sums"), 1)
                pe.wait_ge(sem("latents"), 3)
                for h in range(HEADS):
                    if h >= 2:
                        pe.wait_ge(sem("q_taken"), h - 1)
                        pe.wait_ge(sem("q_rope_taken"), h - 1)
                    at = (NOPE + ROPE) * h
                    for c in range(2):
                        nc.tensor.matmul(bank[h % 2][0:NOPE, 0:T], w_uq[:, c, at:at + NOPE], q_lat[:, c, :], start=(c == 0), stop=(c == 1))
                    for c in range(2):
                        ins = nc.tensor.matmul(bank[2 + h % 2][0:ROPE, 0:T], w_uq[:, c, at + NOPE:at + NOPE + ROPE], q_lat[:, c, :],
                                               start=(c == 0), stop=(c == 1))
                    ins.then_inc(sem("q_ready"), 1)
                    if h >= 2:
                        pe.wait_ge(sem("k_taken"), h - 1)
                    nc.tensor.matmul(bank[4 + h % 2][0:NOPE, 0:T], w_uk[:, NOPE * h:NOPE * h + NOPE], kv_lat[:, :],
                                     start=True, stop=True).then_inc(sem("k_ready"), 1)
                for a in range(TT):
                    nc.tensor.matmul(bank[6 + a][:, :], kv_lat[:, P * a:P * a + P], w_uv[:, :], start=True, stop=True).then_inc(sem("v_ready"), 1)
                pe.wait_ge(sem("q_rope_taken"), HEADS)
                pe.wait_ge(sem("q_taken"), HEADS)
                pe.wait_ge(sem("k_taken"), HEADS)
                rot = const("rot_mla")[0:ROPE, :]
                for j in range(4):
                    nc.tensor.matmul(bank[j][0:ROPE, :], rot, q_rope[:, 2 * j:2 * j + 2, :].rearrange("p a t -> p (a t)"),
                                     start=True, stop=True).then_inc(sem("partners"), 1)
                nc.tensor.matmul(bank[4][0:ROPE, 0:T], rot, k_rot[:, :], start=True, stop=True).then_inc(sem("partners"), 1)
                pe.wait_ge(sem("rotated"), 2)
                att_pe(pe, S,
                       lambda h, a: [(q_nope[:, h, P * a:P * a + P], k_nope[:, h, :]), (q_rope[:, h, P * a:P * a + P], k_rot[:, :])],
                       lambda h, a: v_nat[:, a, VDIM * h:VDIM * h + VDIM])
                pe.wait_ge(sem("out_squares"), 1)
                for c in range(4):
                    ins = nc.tensor.matmul(bank[6][:, 0:T], ones, sq[:, c, :], start=(c == 0), stop=(c == 3))
                ins.then_inc(sem("sums"), 1)

            @S.block.scalar
            def _(act):
                st = Steps(act, sem, "act_step")
                st.tell(nc.scalar.activation(sq[:, 0:2, :], q_lat[:, :, :], ACT.Square), "squares")
                st.tell(nc.scalar.activation(sq[:, 2, :], kv_lat[:, :], ACT.Square), "squares")
                act.wait_ge(sem("sums"), 1)
                st.tell(nc.scalar.activation(root[:, 0, :], bank[6][:, 0:T], ACT.Sqrt, bias=1e-6, scale=1.0 / QLORA), "roots")
                st.tell(nc.scalar.activation(root[:, 1, :], bank[7][:, 0:T], ACT.Sqrt, bias=1e-6, scale=1.0 / KVLORA), "roots")
                act.wait_ge(sem("angles_ready"), 1)
                st.tell(nc.scalar.activation(tab[:, 2, :], tab[:, 2, :], ACT.Sin), "tables")
                st.tell(nc.scalar.activation(tab[:, 3, :], tab[:, 3, :], ACT.Sin), "tables")
                for h in range(HEADS):
                    act.wait_ge(sem("q_ready"), h + 1)
                    st.tell(nc.scalar.activation(q_nope[:, h, :], bank[h % 2][0:NOPE, 0:T], ACT.Copy), "q_taken")
                    act.wait_ge(sem("k_ready"), h + 1)
                    st.tell(nc.scalar.activation(k_nope[:, h, :], bank[4 + h % 2][0:NOPE, 0:T], ACT.Copy), "k_taken")
                att_act(act, st, S)
                act.wait_ge(sem("out_taken"), 4)
                st.tell(nc.scalar.activation(sq[:, :, :], hT[:, 0:4, :], ACT.Square), "out_squares")
                act.wait_ge(sem("sums"), 2)
                st.tell(nc.scalar.activation(root[:, 0, :], bank[6][:, 0:T], ACT.Sqrt, bias=1e-6, scale=1.0 / 512), "roots")

            @S.block.vector
            def _(dve):
                st = Steps(dve, sem, "dve_step")
                dve.wait_ge(small, 16 * 5)
                st.step(nc.vector.tensor_copy(posf[:, :], posi[:, :]))
                rope_tables(dve, st, posf[:, :], const("freq_mla")[0:ROPE, :], tab[:, 0, :], tab[:, 1, :], tab[:, 2, :], tab[:, 3, :])
                dve.wait_ge(sem("roots"), 2)
                st.step(nc.vector.reciprocal(root[:, :, :], root[:, :, :]))
                for c in range(2):
                    st.tell(nc.vector.scalar_tensor_tensor(q_lat[:, c, :], q_lat[:, c, :], par("q_norm_g", c), root[:, 0, :],
                                                           ALU.mult, ALU.mult), "latents")
                st.tell(nc.vector.scalar_tensor_tensor(kv_lat[:, :], kv_lat[:, :], par("kv_norm_g"), root[:, 1, :],
                                                       ALU.mult, ALU.mult), "latents")
                for h in range(HEADS):
                    dve.wait_ge(sem("q_ready"), h + 1)
                    st.step(nc.vector.tensor_copy(q_rope[:, h, :], bank[2 + h % 2][0:ROPE, 0:T]), "q_rope_taken")
                for a in range(TT):
                    dve.wait_ge(sem("v_ready"), a + 1)
                    st.tell(nc.vector.tensor_copy(v_nat[:, a, :], bank[6 + a][:, :]), "v_taken")
                dve.wait_ge(sem("tables"), 2)
                cos4 = tab[:, 2:3, :].to_broadcast([ROPE, HEADS, T])
                sin2 = tab[:, 3:4, :].to_broadcast([ROPE, 2, T])
                dve.wait_ge(sem("partners"), 5)
                st.step(nc.vector.tensor_tensor(q_rope[:, :, :], q_rope[:, :, :], cos4, ALU.mult))
                for j in range(4):
                    st.step(nc.vector.tensor_tensor(tmp[:, 2 * j:2 * j + 2, :], bank[j][0:ROPE, :].rearrange("p (a t) -> p a t", a=2),
                                                    sin2, ALU.mult))
                st.tell(nc.vector.tensor_tensor(q_rope[:, :, :], q_rope[:, :, :], tmp[:, :, :], ALU.add), "rotated")
                st.step(nc.vector.tensor_tensor(tab[:, 0, :], bank[4][0:ROPE, 0:T], tab[:, 3, :], ALU.mult))
                st.step(nc.vector.tensor_tensor(k_rot[:, :], k_rot[:, :], tab[:, 2, :], ALU.mult))
                st.tell(nc.vector.tensor_tensor(k_rot[:, :], k_rot[:, :], tab[:, 0, :], ALU.add), "rotated")
                att_dve(dve, st, S, lambda h: causal, lambda pair: hT[:, pair, :])
                dve.wait_ge(sem("roots"), 3)
                st.step(nc.vector.reciprocal(root[:, 0, :], root[:, 0, :]))
                for c in range(4):
                    nc.vector.scalar_tensor_tensor(hT[:, c, :], hT[:, c, :], par("mla_out_g", c), root[:, 0, :], ALU.mult, ALU.mult)
        if stop == "mla":
            return
        mla.close()


        rwkv = block1.enter_context(ExitStack())
        rc = sb("rwkv_const", [P, RWKV_N], where=rwkv)
        alpha_rho = sb("alpha_rho", [P, HP, 2, T], where=rwkv)
        beta = sb("beta", [P, HP, T], where=rwkv)
        gate = sb("gate", [P, HP, T], where=rwkv)
        bonus = sb("bonus", [P, HP, T], where=rwkv)
        nat = sb("nat", [P, 4, TT, RW], where=rwkv)
        chunk_decay = sb("chunk_decay", [P, HP, NCH], where=rwkv)
        kappa = ps[:, 4:8, :]
        ring_scratch = [ring[:, U_WO % RING + j // 2, 1024 * (j % 2):1024 * (j % 2) + 1024] for j in range(8)]

        def rconst(name):
            at, n = RWKV_AT[name]
            return rc[:, at:at + n]

        def flat(ap):
            return ap.rearrange("p a t -> p (a t)")

        with ExitStack() as c4, Stage(nc, pool) as S:
            sem = S.sem
            lora = sb("lora", [P, RW], where=c4)
            g2 = sb("g2", [P, RW], where=c4)
            sig, csum, iclr, kk, e0, e1, e2, sq = ring_scratch
            r, k, v = ps[:, 0:4, :], ps[:, 4:8, :], ps[:, 8:12, :]
            three = lambda ap: ap.rearrange("p (a t) -> p a t", t=T)

            @S.block.sync
            def _(sp):
                sp.dma_start(rc[:, :], A["const_rwkv"]).then_inc(sem("const_loaded"), 16)
                sp.dma_start(lora[0:64, :], A["rwkv_w2"][0]).then_inc(sem("lora_loaded"), 16)
                sp.dma_start(lora[64:128, :], A["rwkv_a2"][0]).then_inc(sem("lora_loaded"), 16)
                sp.dma_start(g2[:, :], A["rwkv_g2"][0]).then_inc(sem("lora_loaded"), 16)

            @S.block.tensor
            def _(pe):
                pe.wait_ge(sem("lora_loaded"), 48)
                pe.wait_ge(sem("lora_acted"), 2)
                for m in range(HP):
                    nc.tensor.matmul(bank[m // 2][:, T * (m % 2):T * (m % 2) + T], lora[0:64, P * m:P * m + P], ps[0:64, 12, :],
                                     start=True, stop=True).then_inc(sem("decay_ready"), 1)
                for m in range(HP):
                    nc.tensor.matmul(bank[2 + m // 2][:, T * (m % 2):T * (m % 2) + T], lora[64:128, P * m:P * m + P], ps[64:128, 12, :],
                                     start=True, stop=True).then_inc(sem("iclr_ready"), 1)
                for m in range(HP):
                    ins = nc.tensor.matmul(bank[4 + m // 2][:, T * (m % 2):T * (m % 2) + T], g2[:, P * m:P * m + P], ps[:, 13, :],
                                           start=True, stop=True)
                ins.then_inc(sem("gate_ready"), 1)
                pe.wait_ge(sem("squares"), 1)
                for j in range(2):
                    ins = nc.tensor.matmul(bank[6 + j][:, :], heads64, sq[:, 512 * j:512 * j + 512], start=True, stop=True)
                ins.then_inc(sem("norms"), 1)
                pe.wait_ge(sem("rk_ready"), 1)
                pe.wait_ge(sem("gate_taken"), 1)
                for j in range(2):
                    ins = nc.tensor.matmul(bank[4 + j][:, :], heads64, sq[:, 512 * j:512 * j + 512], start=True, stop=True)
                ins.then_inc(sem("bonus_ready"), 1)
                order = [(3, lambda m: v[:, m, :], None), (0, lambda m: alpha_rho[:, m, 0, :], 1), (1, lambda m: beta[:, m, :], 2),
                         (2, lambda m: kappa[:, m, :], 3)]
                n = 0
                for which, src, need in order:
                    if need:
                        pe.wait_ge(sem("factors"), need)
                    for a in range(TT):
                        if n == 0:
                            pe.wait_ge(sem("acts_done"), 2)
                        if n >= 4:
                            pe.wait_ge(sem("nat_taken"), n - 3)
                        for m in range(HP):
                            ins = nc.tensor.transpose(bank[n % 4][:, P * m:P * m + P], src(m)[:, P * a:P * a + P], ident)
                        ins.then_inc(sem("nat_ready"), 1)
                        n += 1

            @S.block.scalar
            def _(act):
                st = Steps(act, sem, "act_step")
                st.tell(nc.scalar.activation(ps[0:64, 12, :], ps[0:64, 12, :], ACT.Tanh), "lora_acted")
                st.tell(nc.scalar.activation(ps[:, 13, :], ps[:, 13, :], ACT.Sigmoid), "lora_acted")
                for m in range(HP):
                    act.wait_ge(sem("decay_ready"), m // 2 * 2 + 2)
                    ins = nc.scalar.activation(sig[:, T * m:T * m + T], bank[m // 2][:, T * (m % 2):T * (m % 2) + T], ACT.Sigmoid,
                                               bias=par("rwkv_w0", m))
                st.tell(ins, "acts_done")
                for m in range(HP):
                    act.wait_ge(sem("iclr_ready"), m // 2 * 2 + 2)
                    ins = nc.scalar.activation(iclr[:, T * m:T * m + T], bank[2 + m // 2][:, T * (m % 2):T * (m % 2) + T], ACT.Sigmoid,
                                               bias=par("rwkv_a0", m))
                st.tell(ins, "acts_done")
                act.wait_ge(sem("kk_raw"), 1)
                st.tell(nc.scalar.activation(sq, kk, ACT.Square), "squares")
                act.wait_ge(sem("csum_ready"), 2)
                st.tell(nc.scalar.activation(e1, csum, ACT.Exp, scale=-EXP_M05), "exps")
                st.tell(nc.scalar.activation(e2, csum, ACT.Exp, scale=EXP_M05), "exps")
                st.tell(nc.scalar.activation(e0, e0, ACT.Exp, scale=-EXP_M05), "exps")
                act.wait_ge(sem("norms"), 1)
                act.wait_ge(sem("csum_used"), 1)
                for j in range(2):
                    ins = nc.scalar.activation(sig[:, 512 * j:512 * j + 512], bank[6 + j][:, :], ACT.Sqrt)
                st.tell(ins, "roots")
                for n in range(8):
                    which = (3, 0, 1, 2)[n // 2]
                    act.wait_ge(sem("nat_ready"), n + 1)
                    st.tell(nc.scalar.activation(nat[:, which, n % 2, :], bank[n % 4][:, :], ACT.Copy), "nat_taken")

            @S.block.vector
            def _(dve):
                st = Steps(dve, sem, "dve_step")
                for m in range(HP):
                    ins = nc.vector.tensor_scalar(kk[:, T * m:T * m + T], k[:, m, :], par("rwkv_k_k", m), None, ALU.mult)
                st.step(ins, "kk_raw")
                dve.wait_ge(sem("const_loaded"), 16)
                dve.wait_ge(sem("acts_done"), 1)
                st.step(nc.vector.tensor_tensor_scan(csum, rconst("no_start"), sig, 0.0, ALU.mult, ALU.add), "csum_ready")
                st.step(nc.vector.tensor_tensor(e0, csum, sig, ALU.subtract), "csum_ready")
                st.tell(nc.vector.memset(bonus[:, 0, 0:1], 0.0), "csum_used")
                dve.wait_ge(sem("gate_ready"), 1)
                for j in range(2):
                    ins = nc.vector.tensor_copy(flat(gate[:, 2 * j:2 * j + 2, :]), bank[4 + j][:, :])
                st.tell(ins, "gate_taken")
                dve.wait_ge(sem("acts_done"), 2)
                for m in range(HP):
                    ins = nc.vector.tensor_scalar(beta[:, m, :], iclr[:, T * m:T * m + T], 1.0, par("rwkv_k_a", m), ALU.subtract, ALU.mult)
                st.step(ins)
                st.step(nc.vector.scalar_tensor_tensor(flat(k), flat(beta[:, :, :]), 1.0, flat(k), ALU.add, ALU.mult))
                dve.wait_ge(sem("norms"), 1)
                for m in range(HP):
                    ins = nc.vector.scalar_tensor_tensor(sq[:, T * m:T * m + T], r[:, m, :], par("rwkv_r_k", m), k[:, m, :], ALU.mult, ALU.mult)
                st.tell(ins, "rk_ready")
                dve.wait_ge(sem("roots"), 1)
                st.step(nc.vector.tensor_scalar(sig, sig, 1e-12, None, ALU.max))
                st.step(nc.vector.reciprocal(sig, sig))
                st.step(nc.vector.tensor_tensor(kk, kk, sig, ALU.mult))
                dve.wait_ge(sem("exps"), 3)
                st.tell(nc.vector.scalar_tensor_tensor(alpha_rho[:, :, 0, :], three(kk), -1.0, three(e0), ALU.mult, ALU.mult), "factors")
                st.step(nc.vector.tensor_tensor(kk, kk, iclr, ALU.mult))
                st.tell(nc.vector.tensor_tensor(flat(beta[:, :, :]), kk, e2, ALU.mult), "factors")
                st.tell(nc.vector.tensor_tensor(flat(k), flat(k), e2, ALU.mult), "factors")
                nc.vector.tensor_tensor(alpha_rho[:, :, 1, :], r, three(e1), ALU.mult)
                nc.vector.tensor_copy(chunk_decay[:, :, :], three(e1)[:, :, CH - 1:T:CH])
                dve.wait_ge(sem("bonus_ready"), 1)
                for j in range(2):
                    nc.vector.tensor_tensor(flat(bonus[:, 2 * j:2 * j + 2, :]), bank[4 + j][:, :], flat(v[:, 2 * j:2 * j + 2, :]), ALU.mult)
        if stop == "rwkv_prep":
            return

        NS = 8
        for half in range(2):
            with ExitStack() as c5, Stage(nc, pool) as S:
                sem = S.sem
                mats = [x.rearrange("p (s t) -> p s t", t=P) for x in ring_scratch]
                lt, a3, a2, a4, low, inv_t, inv, low_b = mats
                xs = lt
                a2v = sb("a2v", [P, NS, 64], where=c5)
                za = low_b
                ta_t = sb("ta_t", [P, 2, T], where=c5)
                step_m = sb("step_m", [P, NCH, 2, P], where=c5)
                step_n = sb("step_n", [P, NCH, 2, 64], where=c5)
                state = sb("state", [P, 2, 2, 64], where=c5)
                plus = sb("plus", [P, 2, 64], where=c5)
                states = sb("states", [P, NCH, 2, P], where=c5)
                us = sb("us", [P, TT, 2, 2, 64], where=c5)
                systems = [(par_, hp, a) for par_ in range(2) for hp in range(2) for a in range(TT)]
                where = {sy: i for i, sy in enumerate(systems)}
                LEVELS = (2, 4, 8, 16, 32)

                def head_cols(h2, hp):
                    return slice(P * (2 * half + hp) + 64 * h2, P * (2 * half + hp) + 64 * h2 + 64)

                @S.block.gpsimd
                def _(gps):
                    nc.gpsimd.memset(step_m[:, :, :, :], 0.0)
                    nc.gpsimd.memset(states[:, :, :, :], 0.0).then_inc(sem("cleared"), 1)
                    gps.wait_ge(sem("low_ready"), 2)
                    for n, b in enumerate(LEVELS):
                        for q in range(2):
                            if n:
                                gps.wait_ge(sem("x_ready"), 2 * (n - 1) + q + 1)
                            nc.gpsimd.tensor_tensor(low_b[:, 4 * q:4 * q + 4, :], low[:, 4 * q:4 * q + 4, :],
                                                    rconst(f"lower{b}").unsqueeze(1).to_broadcast([P, 4, P]), ALU.mult
                                                    ).then_inc(sem("low_b_ready"), 1)

                @S.block.tensor
                def _(pe):
                    def token(a):
                        return slice(P * a, P * a + P)

                    for src, b0 in ((beta, 0), (kappa, 4)):
                        for h2 in range(2):
                            for hp in range(2):
                                for a in range(TT):
                                    rows = slice(64 * h2, 64 * h2 + 64)
                                    ins = nc.tensor.matmul(bank[b0 + 2 * h2 + hp][:, T * a:T * a + T], src[rows, 2 * half + hp, token(a)],
                                                           alpha_rho[rows, 2 * half + hp, :, token(a)], start=True, stop=True)
                                ins.then_inc(sem("products"), 1)
                    for h2 in range(2):
                        pe.wait_ge(sem("products_taken"), 2 * h2 + 1)
                        for hp in range(2):
                            for a in range(TT):
                                rows = slice(64 * h2, 64 * h2 + 64)
                                at = P * (2 * hp + a)
                                ins = nc.tensor.matmul(bank[2 * h2][:, at:at + P], alpha_rho[rows, 2 * half + hp, 0, token(a)],
                                                       beta[rows, 2 * half + hp, token(a)], start=True, stop=True)
                        ins.then_inc(sem("low_product"), 1)
                    for n, b in enumerate(LEVELS):
                        for q in range(2):
                            pe.wait_ge(sem("low_b_ready"), 2 * n + q + 1)
                            pe.wait_ge(sem("inv_ready"), 2 * n + q + 1)
                            if n == 0:
                                pe.wait_ge(sem("low_ready"), q + 1)
                            for j in range(4):
                                ins = nc.tensor.matmul(bank[q][:, P * j:P * j + P], low_b[:, 4 * q + j, :], inv_t[:, 4 * q + j, :],
                                                       start=True, stop=True)
                            ins.then_inc(sem("x_ready"), 1)
                        for q in range(2):
                            pe.wait_ge(sem("x_taken"), 2 * n + q + 1)
                            if n == 0:
                                pe.wait_ge(sem("products_taken"), 8)
                            for j in range(4):
                                s_ = 4 * q + j
                                ins = nc.tensor.matmul(bank[2 + q][:, P * j:P * j + P], inv[:, s_, :], xs[:, s_, :], start=True, stop=True)
                            if b != LEVELS[-1]:
                                for j in range(4):
                                    s_ = 4 * q + j
                                    ins = nc.tensor.matmul(bank[4 + q][:, P * j:P * j + P], xs[:, s_, :], inv[:, s_, :], start=True, stop=True)
                            ins.then_inc(sem("growth"), 1)
                    for q in range(2):
                        for j in range(4):
                            h2, hp, a = systems[4 * q + j]
                            ins = nc.tensor.matmul(bank[6 + q][:, 64 * j:64 * j + 64], a2[:, 4 * q + j, :], nat[:, 3, a, head_cols(h2, hp)],
                                                   start=True, stop=True)
                        ins.then_inc(sem("a2v_ready"), 1)
                    for q in range(2):
                        pe.wait_ge(sem("inv_ready"), 2 * len(LEVELS) + q + 1)
                        pe.wait_ge(sem("a2v_taken"), q + 1)
                        for j in range(4):
                            h2, hp, a = systems[4 * q + j]
                            nc.tensor.matmul(bank[q][:, P * j:P * j + 64], inv_t[:, 4 * q + j, :], nat[:, 0, a, head_cols(h2, hp)],
                                             start=True, stop=True)
                            ins = nc.tensor.matmul(bank[q][:, P * j + 64:P * j + P], inv_t[:, 4 * q + j, :], a2v[:, 4 * q + j, :],
                                                   start=True, stop=True)
                        ins.then_inc(sem("za_ready"), 1)
                    for s_, (h2, hp, a) in enumerate(systems):
                        at = T * hp + P * a
                        ins = nc.tensor.matmul(bank[4][64 * h2:64 * h2 + 64, at:at + P], nat[:, 0, a, head_cols(h2, hp)], inv_t[:, s_, :],
                                               start=True, stop=True)
                    ins.then_inc(sem("ta_ready"), 1)
                    pe.wait_ge(sem("za_taken"), 2)
                    for ph in range(2):
                        rows = slice(64 * ph, 64 * ph + 64)
                        for s_, (h2, hp, a) in enumerate(systems):
                            at = 64 * (2 * a + hp)
                            ins = nc.tensor.matmul(bank[5 + ph][64 * h2:64 * h2 + 64, at:at + 64], za[rows, s_, 0:64],
                                                   nat[rows, 1, a, head_cols(h2, hp)], start=True, stop=True)
                        ins.then_inc(sem("m_ready"), 1)
                    for ph in range(2):
                        rows = slice(64 * ph, 64 * ph + 64)
                        o = bank[7 if ph == 0 else 0]
                        for s_, (h2, hp, a) in enumerate(systems):
                            at = 64 * (2 * a + hp)
                            dst = o[64 * h2:64 * h2 + 64, at:at + 64]
                            nc.tensor.matmul(dst, nat[rows, 1, a, head_cols(h2, hp)], za[rows, s_, 64:P], start=True, stop=False)
                            ins = nc.tensor.matmul(dst, nat[rows, 2, a, head_cols(h2, hp)], nat[rows, 3, a, head_cols(h2, hp)],
                                                   start=False, stop=True)
                        ins.then_inc(sem("n_ready"), 1)
                    pe.wait_ge(sem("m_taken"), 4)
                    for c in range(1, NCH - 1):
                        pe.wait_ge(sem("state_ready"), c)
                        for hp in range(2):
                            ins = nc.tensor.matmul(bank[1 + c % 2][:, 64 * hp:64 * hp + 64], step_m[:, c, hp, :], state[:, c % 2, hp, :],
                                                   start=True, stop=True)
                        ins.then_inc(sem("m_state"), 1)
                    pe.wait_ge(sem("states_ready"), 2 * (NCH - 1))
                    pe.wait_ge(sem("ta_taken"), 1)
                    for c in range(NCH):
                        a, ph = c // 2, c % 2
                        for hp in range(2):
                            at = P * (2 * a + hp)
                            ins = nc.tensor.matmul(bank[3][64 * ph:64 * ph + 64, at:at + P], ta_t[:, hp, CH * c:CH * c + CH],
                                                   states[:, c, hp, :], start=True, stop=True)
                    ins.then_inc(sem("u_ready"), 1)
                    for hp in range(2):
                        if hp == 0:
                            pe.wait_ge(sem("ta_taken"), 1)
                            pe.wait_ge(sem("m_taken"), 4)
                        o = bank[4 + hp]
                        for c in range(NCH):
                            nc.tensor.matmul(o[:, CH * c:CH * c + CH], states[:, c, hp, :], alpha_rho[:, 2 * half + hp, 1, CH * c:CH * c + CH],
                                             start=(c == 0), stop=False, skip_group_check=True)
                        if hp == 0:
                            pe.wait_ge(sem("u_taken"), 2)
                        for h2 in range(2):
                            for a in range(TT):
                                s_ = where[(h2, hp, a)]
                                dst = o[64 * h2:64 * h2 + 64, token(a)]
                                nc.tensor.matmul(dst, us[:, a, hp, h2, :], a3[:, s_, :], start=False, stop=False, skip_group_check=True)
                                ins = nc.tensor.matmul(dst, nat[:, 3, a, head_cols(h2, hp)], a4[:, s_, :], start=False,
                                                       stop=True, skip_group_check=True)
                        ins.then_inc(sem("o_ready"), 1)

                @S.block.scalar
                def _(act):
                    st = Steps(act, sem, "act_step")
                    for n in range(len(LEVELS)):
                        for q in range(2):
                            act.wait_ge(sem("x_ready"), 2 * n + q + 1)
                            if n:
                                act.wait_ge(sem("growth"), 2 * (n - 1) + q + 1)
                            else:
                                act.wait_ge(sem("inv_ready"), 2)
                            st.tell(nc.scalar.activation(flat(xs[:, 4 * q:4 * q + 4, :]), bank[q][:, :], ACT.Copy), "x_taken")
                    for q in range(2):
                        act.wait_ge(sem("a2v_ready"), q + 1)
                        st.tell(nc.scalar.activation(flat(a2v[:, 4 * q:4 * q + 4, :]), bank[6 + q][:, 0:T], ACT.Copy), "a2v_taken")
                    act.wait_ge(sem("ta_ready"), 1)
                    st.tell(nc.scalar.activation(flat(ta_t[:, :, :]), bank[4][:, :], ACT.Copy), "ta_taken")
                    act.wait_ge(sem("cleared"), 1)
                    for ph in range(2):
                        act.wait_ge(sem("m_ready"), ph + 1)
                        for h2 in range(2):
                            rows = slice(64 * h2, 64 * h2 + 64)
                            for a in range(TT):
                                ins = nc.scalar.activation(step_m[rows, 2 * a + ph, :, rows],
                                                           bank[5 + ph][rows, P * a:P * a + P].rearrange("p (h j) -> p h j", h=2), ACT.Copy)
                            st.tell(ins, "m_taken")
                    for c in range(1, NCH):
                        act.wait_ge(sem("state_ready"), c)
                        for h2 in range(2):
                            rows = slice(64 * h2, 64 * h2 + 64)
                            st.tell(nc.scalar.activation(states[rows, c, :, rows], state[rows, c % 2, :, :], ACT.Copy), "states_ready")
                    for hp in range(2):
                        act.wait_ge(sem("o_ready"), hp + 1)
                        nc.scalar.activation(hT[:, 4 + 2 * half + hp, :], bank[4 + hp][:, 0:T], ACT.Copy)

                @S.block.vector
                def _(dve):
                    st = Steps(dve, sem, "dve_step")
                    above = rconst("above").unsqueeze(1).to_broadcast([P, TT, P])
                    above_eq = rconst("above_eq").unsqueeze(1).to_broadcast([P, TT, P])
                    for which, b0 in enumerate((0, 4)):
                        strict, full = ((lt, a3), (a2, a4))[which]
                        for h2 in range(2):
                            for hp in range(2):
                                dve.wait_ge(sem("products"), 4 * which + 2 * h2 + hp + 1)
                                b = bank[b0 + 2 * h2 + hp][:, :].rearrange("p (a x t) -> p a x t", a=TT, x=2)
                                s_ = 4 * h2 + 2 * hp
                                nc.vector.tensor_tensor(strict[:, s_:s_ + 2, :], b[:, :, 0, :], above, ALU.mult)
                                st.tell(nc.vector.tensor_tensor(full[:, s_:s_ + 2, :], b[:, :, 1, :], above_eq, ALU.mult), "products_taken")
                        if which == 0:
                            dve.wait_ge(sem("products_taken"), 4)
                            for q in range(2):
                                dve.wait_ge(sem("low_product"), q + 1)
                                st.step(nc.vector.tensor_tensor(low[:, 4 * q:4 * q + 4, :], bank[2 * q][:, :].rearrange("p (s t) -> p s t", s=4),
                                                                rconst("below").unsqueeze(1).to_broadcast([P, 4, P]), ALU.mult), "low_ready")
                    for q in range(2):
                        part = slice(4 * q, 4 * q + 4)
                        ident4 = ident.unsqueeze(1).to_broadcast([P, 4, P])
                        st.step(nc.vector.tensor_tensor(inv[:, part, :], low[:, part, :], rconst("lower1").unsqueeze(1).to_broadcast([P, 4, P]), ALU.mult))
                        st.step(nc.vector.tensor_tensor(inv[:, part, :], inv[:, part, :], ident4, ALU.add))
                        st.step(nc.vector.tensor_tensor(inv_t[:, part, :], lt[:, part, :], rconst("lower1_t").unsqueeze(1).to_broadcast([P, 4, P]), ALU.mult))
                        st.step(nc.vector.tensor_tensor(inv_t[:, part, :], inv_t[:, part, :], ident4, ALU.add), "inv_ready")
                    for n, b in enumerate(LEVELS):
                        for q in range(2):
                            dve.wait_ge(sem("growth"), 2 * n + q + 1)
                            part = slice(4 * q, 4 * q + 4)
                            if b != LEVELS[-1]:
                                nc.vector.tensor_tensor(flat(inv[:, part, :]), bank[4 + q][:, :], flat(inv[:, part, :]), ALU.add)
                            st.step(nc.vector.tensor_tensor(flat(inv_t[:, part, :]), bank[2 + q][:, :], flat(inv_t[:, part, :]), ALU.add), "inv_ready")
                    for q in range(2):
                        dve.wait_ge(sem("za_ready"), q + 1)
                        st.tell(nc.vector.tensor_copy(flat(za[:, 4 * q:4 * q + 4, :]), bank[q][:, :]), "za_taken")
                    for ph in range(2):
                        dve.wait_ge(sem("n_ready"), ph + 1)
                        o = bank[7 if ph == 0 else 0]
                        st.step(nc.vector.tensor_copy(step_n[:, ph:NCH:2, :, :].rearrange("p c h i -> p c (h i)"),
                                                      o[:, 0:T].rearrange("p (c x) -> p c x", c=2)))
                    for c in range(NCH - 1):
                        now, new = state[:, c % 2, :, :], state[:, (c + 1) % 2, :, :]
                        decay = chunk_decay[:, 2 * half:2 * half + 2, c:c + 1].to_broadcast([P, 2, 64])
                        if c == 0:
                            st.step(nc.vector.tensor_tensor(new, step_n[:, 0, :, :], decay, ALU.mult), "state_ready")
                            continue
                        st.step(nc.vector.tensor_tensor(plus[:, :, :], now, step_n[:, c, :, :], ALU.add))
                        dve.wait_ge(sem("m_state"), c)
                        st.step(nc.vector.tensor_tensor(plus[:, :, :], bank[1 + c % 2][:, 0:P].rearrange("p (h i) -> p h i", h=2), plus[:, :, :], ALU.add))
                        if c >= 1:
                            dve.wait_ge(sem("states_ready"), 2 * (c - 1))
                        st.step(nc.vector.tensor_tensor(new, plus[:, :, :], decay, ALU.mult), "state_ready")
                    dve.wait_ge(sem("u_ready"), 1)
                    for h2 in range(2):
                        for a in range(TT):
                            ins = nc.vector.tensor_tensor(us[:, a, :, h2, :], bank[3][:, 2 * P * a:2 * P * a + 2 * P].rearrange("p (h x i) -> p h x i", h=2, x=2)[:, :, h2, :],
                                                          za[:, 4 * h2 + a:4 * h2 + a + 3:2, 64:P], ALU.add)
                        st.tell(ins, "u_taken")
            if stop == f"rwkv{half}":
                return

        with ExitStack() as c6, Stage(nc, pool) as S:
            sem = S.sem
            o = hT[:, 4:8, :]
            sq = sb("sq", [P, HP, T], where=c6)

            @S.block.sync
            def _(sp):
                for n, u in enumerate(range(U_WO, U_WO + WO_UNITS)):
                    load_unit(sp, u, slot3(u, DC), cols8(A["w_o"][0], 256 * n))

            @S.block.tensor
            def _(pe):
                for j in range(2):
                    nc.tensor.matmul(bank[j][:, :], heads64, flat(o[:, 2 * j:2 * j + 2, :]), start=True, stop=True).then_inc(sem("means"), 1)
                for j in range(2):
                    pe.wait_ge(sem("squares"), j + 1)
                    nc.tensor.matmul(bank[2 + j][:, :], heads64, flat(sq[:, 2 * j:2 * j + 2, :]), start=True, stop=True).then_inc(sem("vars"), 1)

            @S.block.scalar
            def _(act):
                for j in range(2):
                    act.wait_ge(sem("centered"), j + 1)
                    nc.scalar.activation(flat(sq[:, 2 * j:2 * j + 2, :]), flat(o[:, 2 * j:2 * j + 2, :]), ACT.Square).then_inc(sem("squares"), 1)
                for j in range(2):
                    act.wait_ge(sem("vars"), j + 1)
                    nc.scalar.activation(flat(sq[:, 2 * j:2 * j + 2, :]), bank[2 + j][:, :], ACT.Sqrt, bias=64e-5, scale=1.0 / 64).then_inc(sem("roots"), 1)

            @S.block.vector
            def _(dve):
                st = Steps(dve, sem, "dve_step")
                for j in range(2):
                    oj = flat(o[:, 2 * j:2 * j + 2, :])
                    dve.wait_ge(sem("means"), j + 1)
                    st.tell(nc.vector.scalar_tensor_tensor(oj, bank[j][:, :], -1.0 / 64, oj, ALU.mult, ALU.add), "centered")
                for j in range(2):
                    oj, sj = flat(o[:, 2 * j:2 * j + 2, :]), flat(sq[:, 2 * j:2 * j + 2, :])
                    dve.wait_ge(sem("roots"), j + 1)
                    st.step(nc.vector.reciprocal(sj, sj))
                    st.step(nc.vector.tensor_tensor(oj, oj, sj, ALU.mult))
                    for m in (2 * j, 2 * j + 1):
                        st.step(nc.vector.tensor_scalar(o[:, m, :], o[:, m, :], par("rwkv_gn_g", m), par("rwkv_gn_b", m), ALU.mult, ALU.add))
                    st.step(nc.vector.tensor_tensor(oj, oj, flat(bonus[:, 2 * j:2 * j + 2, :]), ALU.add))
                    st.step(nc.vector.tensor_tensor(oj, oj, flat(gate[:, 2 * j:2 * j + 2, :]), ALU.mult))
        if stop == "rwkv":
            return
        rwkv.close()
        block1.close()


        def layer_norm(S, x, g, b, root, sq, banks, after=None):
            sem = S.sem
            mean, var = bank[banks[0]][:, 0:T], bank[banks[1]][:, 0:T]

            def tensor(pe):
                for c in range(DC):
                    pe.wait_ge(sem("x_ready"), c + 1)
                    ins = nc.tensor.matmul(mean, ones, x[:, c, :], start=(c == 0), stop=(c == DC - 1))
                ins.then_inc(sem("mean_ready"), 1)
                for c in range(DC):
                    if c % 4 == 0:
                        pe.wait_ge(sem("squares"), c // 4 + 1)
                    ins = nc.tensor.matmul(var, ones, sq[:, c, :], start=(c == 0), stop=(c == DC - 1))
                ins.then_inc(sem("var_ready"), 1)

            def scalar(act):
                for j in range(2):
                    act.wait_ge(sem("centered"), j + 1)
                    nc.scalar.activation(sq[:, 4 * j:4 * j + 4, :], x[:, 4 * j:4 * j + 4, :], ACT.Square).then_inc(sem("squares"), 1)
                act.wait_ge(sem("var_ready"), 1)
                nc.scalar.activation(root, var, ACT.Sqrt, bias=1e-5, scale=1.0 / D).then_inc(sem("root_ready"), 1)
                for c in range(DC):
                    act.wait_ge(sem("scaled"), c + 1)
                    nc.scalar.activation(x[:, c, :], x[:, c, :], ACT.Identity, bias=par(b, c)).then_inc(sem("normed"), 1)

            def vector(dve, st):
                dve.wait_ge(sem("mean_ready"), 1)
                for j in range(2):
                    xj = x[:, 4 * j:4 * j + 4, :]
                    st.step(nc.vector.scalar_tensor_tensor(xj, mean.unsqueeze(1).to_broadcast([P, 4, T]), -1.0 / D, xj, ALU.mult, ALU.add), "centered")
                dve.wait_ge(sem("root_ready"), 1)
                st.step(nc.vector.reciprocal(root, root))
                for c in range(DC):
                    st.tell(nc.vector.scalar_tensor_tensor(x[:, c, :], x[:, c, :], par(g, c), root, ALU.mult, ALU.mult), "scaled")

            return tensor, scalar, vector

        moe = ctx.enter_context(ExitStack())
        h_nat = sb("h_nat", [P, TT, D], where=moe)
        rank = sb("rank", [P, TT, E], where=moe)
        gates = sb("gates", [P, TT, E], where=moe)
        b1_pad = sb("b1_pad", [P, 2 * F_E], where=moe)
        passes = sb("passes", [P, 1], I32, where=moe)
        acc = hT

        with ExitStack() as c7, Stage(nc, pool) as S:
            sem = S.sem
            sq = sb("sq", [P, DC, T], where=c7)
            root = sb("root", [P, T], where=c7)
            w_r = sb("w_r", [P, DC, E], where=c7)
            b_r = sb("b_r", [P, E], where=c7)
            b2 = sb("b2", [E, D], where=c7)
            logits = sb("logits", [P, TT, E], where=c7)
            work = sb("work", [P, TT, E], where=c7)
            hit = sb("hit", [P, TT, E], where=c7)
            chosen = sb("chosen", [P, TT, E], where=c7)
            top = sb("top", [P, TT, TOPK + 1], where=c7)
            gates_t = sb("gates_t", [E, T], where=c7)
            most = sb("most", [P, 4], where=c7)
            ln_pe, ln_act, ln_dve = layer_norm(S, xT, "ln1_g", "ln1_b", root[:, :], sq, (2, 3))

            @S.block.sync
            def _(sp):
                for k in range(EXPERT_UNITS):
                    u = U_EXP + k
                    if k < 8:
                        load_unit(sp, u, ring[:, k, :], A["exp_w1"][0, 0, P * k:P * k + P, :])
                    else:
                        load_unit(sp, u, slot3(k, 2), A["exp_w2"][0, 0, T * (k - 8):T * (k - 8) + T, :].rearrange("(x p) n -> p x n", p=P))

            @S.block.gpsimd
            def _(gps):
                nc.gpsimd.memset(b1_pad[:, :], 0.0).then_inc(sem("b1_cleared"), 1)

            @S.block.tensor
            def _(pe):
                for m in range(DC):
                    if m % 2 == 0:
                        unit_ready(pe, U_WO + m // 2)
                    if m >= 2:
                        pe.wait_ge(sem("x_ready"), m - 1)
                    w = slot3(U_WO + m // 2, DC)
                    for c in range(DC):
                        ins = nc.tensor.matmul(bank[m % 2][:, 0:T], w[:, c, P * (m % 2):P * (m % 2) + P], hT[:, c, :],
                                               start=(c == 0), stop=(c == DC - 1))
                        if c == 0 and m and m % 2 == 0:
                            ins.then_inc(used, 1)
                    ins.then_inc(sem("mix_ready"), 1)
                pe.wait_ge(sem("mix_ready"), DC)
                pe.sem_inc(used, 1)
                ln_pe(pe)
                pe.wait_ge(sem("router_loaded"), 48)
                for a in range(TT):
                    for c in range(DC):
                        if a == 0:
                            pe.wait_ge(sem("h_ready"), c + 1)
                        ins = nc.tensor.matmul(bank[4][:, E * a:E * a + E], hT[:, c, P * a:P * a + P], w_r[:, c, :], start=(c == 0), stop=(c == DC - 1))
                ins.then_inc(sem("logits_ready"), 1)
                for n in range(4):
                    for j in range(4):
                        c = 4 * (n % 2) + j
                        ins = nc.tensor.transpose(bank[n % 2][:, P * j:P * j + P], hT[:, c, P * (n // 2):P * (n // 2) + P], ident)
                    ins.then_inc(sem("h_turned"), 1)
                    if n < 2:
                        pe.wait_ge(sem("h_turned_taken"), n + 1)
                pe.wait_ge(sem("chosen_ready"), 1)
                nc.tensor.matmul(bank[5][:, 0:E], const("before"), chosen[:, 0, :], start=True, stop=True)
                nc.tensor.matmul(bank[5][:, E:2 * E], const("before"), chosen[:, 1, :], start=True, stop=False)
                nc.tensor.matmul(bank[5][:, E:2 * E], ones, chosen[:, 0, :], start=False, stop=True)
                nc.tensor.matmul(bank[5][:, 2 * E:3 * E], ones, chosen[:, 0, :], start=True, stop=False)
                nc.tensor.matmul(bank[5][:, 2 * E:3 * E], ones, chosen[:, 1, :], start=False, stop=True).then_inc(sem("ranks_ready"), 1)
                pe.wait_ge(sem("gates_ready"), 1)
                for a in range(TT):
                    ins = nc.tensor.transpose(bank[6][0:E, P * a:P * a + P], gates[:, a, :], ident)
                ins.then_inc(sem("gates_turned"), 1)
                pe.wait_ge(sem("gates_taken"), 1)
                pe.wait_ge(sem("h_turned"), 4)
                for m in range(DC):
                    if m == 0:
                        pe.wait_ge(sem("h_turned_taken"), 4)
                    if m >= 2:
                        pe.wait_ge(sem("acc_ready"), m - 1)
                    nc.tensor.matmul(bank[m % 2][:, 0:T], b2[:, P * m:P * m + P], gates_t[:, :], start=True, stop=True).then_inc(sem("b2_ready"), 1)

            @S.block.scalar
            def _(act):
                act.dma_start(w_r[:, :, :], A["router_w"][0].rearrange("(c p) e -> p c e", p=P)).then_inc(sem("router_loaded"), 16)
                act.dma_start(b_r[:, :], A["router_b"].to_broadcast([P, E])).then_inc(sem("router_loaded"), 16)
                act.dma_start(b2[:, :], A["exp_b2"][0]).then_inc(sem("router_loaded"), 16)
                act.wait_ge(sem("b1_cleared"), 1)
                act.dma_start(b1_pad[0:E, :], A["exp_b1"][0]).then_inc(sem("b1_loaded"), 16)
                for j in range(2):
                    nc.scalar.activation(xT[:, 4 * j:4 * j + 4, :], xT[:, 4 * j:4 * j + 4, :], ACT.Copy, scale=ALPHA).then_inc(sem("x_scaled"), 1)
                ln_act(act)
                for n in range(4):
                    act.wait_ge(sem("h_turned"), n + 1)
                    nc.scalar.activation(h_nat[:, n // 2, 512 * (n % 2):512 * (n % 2) + 512], bank[n % 2][:, :], ACT.Copy).then_inc(sem("h_turned_taken"), 1)
                act.wait_ge(sem("shifted_logits"), 1)
                nc.scalar.activation(work[:, :, :], work[:, :, :], ACT.Exp).then_inc(sem("exp_ready"), 1)
                act.wait_ge(sem("gates_turned"), 1)
                nc.scalar.activation(gates_t[:, :], bank[6][0:E, 0:T], ACT.Copy).then_inc(sem("gates_taken"), 1)
                act.wait_ge(sem("b1_loaded"), 16)

            @S.block.vector
            def _(dve):
                st = Steps(dve, sem, "dve_step")
                for m in range(DC):
                    dve.wait_ge(sem("mix_ready"), m + 1)
                    dve.wait_ge(sem("x_scaled"), m // 4 + 1)
                    st.tell(nc.vector.scalar_tensor_tensor(xT[:, m, :], bank[m % 2][:, 0:T], mod[:, 16 + m:17 + m], xT[:, m, :],
                                                           ALU.mult, ALU.add), "x_ready")
                dve.wait_ge(sem("x_ready"), DC)
                ln_dve(dve, st)
                for c in range(DC):
                    dve.wait_ge(sem("normed"), c + 1)
                    st.tell(nc.vector.tensor_scalar(hT[:, c, :], xT[:, c, :], mod[:, 32 + c:33 + c], mod[:, 24 + c:25 + c], ALU.mult, ALU.add), "h_ready")
                rev = const("rev").unsqueeze(1).to_broadcast([P, TT, E])
                wide = lambda ap: ap.to_broadcast([P, TT, E])
                dve.wait_ge(sem("logits_ready"), 1)
                dve.wait_ge(sem("router_loaded"), 48)
                st.step(nc.vector.tensor_tensor(logits[:, :, :], bank[4][:, 0:TT * E].rearrange("p (a e) -> p a e", a=TT),
                                                b_r[:, :].unsqueeze(1).to_broadcast([P, TT, E]), ALU.add))
                nc.vector.memset(chosen[:, :, :], 0.0)
                st.step(nc.vector.tensor_copy(work[:, :, :], logits[:, :, :]))
                for k in range(TOPK):
                    st.step(nc.vector.tensor_reduce(top[:, :, k], work[:, :, :], AX_X, ALU.max))
                    st.step(nc.vector.tensor_tensor(hit[:, :, :], work[:, :, :], wide(top[:, :, k:k + 1]), ALU.is_equal))
                    st.step(nc.vector.tensor_tensor(hit[:, :, :], hit[:, :, :], rev, ALU.mult))
                    st.step(nc.vector.tensor_reduce(top[:, :, TOPK], hit[:, :, :], AX_X, ALU.max))
                    st.step(nc.vector.tensor_tensor(hit[:, :, :], rev, wide(top[:, :, TOPK:TOPK + 1]), ALU.is_equal))
                    nc.vector.tensor_tensor(chosen[:, :, :], chosen[:, :, :], hit[:, :, :], ALU.add)
                    st.step(nc.vector.scalar_tensor_tensor(work[:, :, :], hit[:, :, :], NEG, work[:, :, :], ALU.mult, ALU.add))
                st.step(nc.vector.tensor_tensor(work[:, :, :], logits[:, :, :], wide(top[:, :, 0:1]), ALU.subtract), "shifted_logits")
                st.tell(nc.vector.tensor_copy(hit[:, 0, 0:1], top[:, 0, 0:1]), "chosen_ready")
                dve.wait_ge(sem("exp_ready"), 1)
                st.step(nc.vector.tensor_tensor(gates[:, :, :], work[:, :, :], chosen[:, :, :], ALU.mult))
                st.step(nc.vector.tensor_reduce(top[:, :, 1], gates[:, :, :], AX_X, ALU.add))
                st.step(nc.vector.reciprocal(top[:, :, 1], top[:, :, 1]))
                st.tell(nc.vector.tensor_tensor(gates[:, :, :], gates[:, :, :], wide(top[:, :, 1:2]), ALU.mult), "gates_ready")
                dve.wait_ge(sem("ranks_ready"), 1)
                st.step(nc.vector.scalar_tensor_tensor(rank[:, :, :], bank[5][:, 0:TT * E].rearrange("p (a e) -> p a e", a=TT), 1.0, chosen[:, :, :],
                                                       ALU.add, ALU.mult))
                st.step(nc.vector.tensor_scalar(rank[:, :, :], rank[:, :, :], 1.0, None, ALU.subtract))
                st.step(nc.vector.tensor_reduce(most[:, 0:1], bank[5][:, 2 * E:3 * E], AX_X, ALU.max))
                for j in range(1, 4):
                    st.step(nc.vector.tensor_scalar(most[:, j:j + 1], most[:, 0:1], SLOTS * j + 0.5, None, ALU.is_gt))
                st.step(nc.vector.tensor_reduce(most[:, 0:1], most[:, 1:4], AX_X, ALU.add))
                st.step(nc.vector.tensor_scalar(passes[:, :], most[:, 0:1], 1.0, None, ALU.add))
                for m in range(DC):
                    dve.wait_ge(sem("b2_ready"), m + 1)
                    st.tell(nc.vector.tensor_copy(acc[:, m, :], bank[m % 2][:, 0:T]), "acc_ready")
        if stop == "mix_out":
            return

        n_passes = nc.values_load(passes[0:1, 0:1], min_val=1, max_val=T // SLOTS)
        PAIRS = E // 2
        with ExitStack() as c8:
            pick = sb("pick", [P, TT, 2, SLOTS], where=c8)
            pick_gate = sb("pick_gate", [P, TT, 2, SLOTS], where=c8)
            gate_slots = sb("gate_slots", [P, T], where=c8)
            row_e = sb("row_e", [P, 2, SLOTS], where=c8)
            xt = sb("xt", [P, DC, 2 * SLOTS], where=c8)
            glu = sb("glu", [P, 512], where=c8)
            lin = sb("lin", [P, 512], where=c8)
            sg = sb("sg", [P, 512], where=c8)
            ut = sb("ut", [P, 4, P], where=c8)
            y = sb("y", [P, D], where=c8)
            with nc.Fori(0, n_passes) as p, Stage(nc, pool) as S:
                sem = S.sem

                def rounds(i, e2):
                    return p * E + (i * 2 + (e2 + U_EXP // RING))

                @S.block.sync
                def _(sp):
                    def load_expert(e, rnd):
                        for k in range(EXPERT_UNITS):
                            sp.wait_ge(used, (rnd - 1) * RING + (k + 1))
                            if k < 8:
                                dst, src = ring[:, k, :], A["exp_w1"][0, e, P * k:P * k + P, :]
                            else:
                                dst = slot3(k, 2)
                                src = A["exp_w2"][0, e, T * (k - 8):T * (k - 8) + T, :].rearrange("(x p) n -> p x n", p=P)
                            sp.dma_start(dst, src).then_inc(loaded[k], 16)

                    with sp.Fori(1, E) as e:
                        load_expert(e, p * E + (e + U_EXP // RING))
                    with sp.If(p < n_passes - 1):
                        load_expert(0, p * E + (E + U_EXP // RING))

                @S.block.tensor
                def _(pe):
                    pe.sem_inc(sem("back"), 1)
                    with pe.Fori(0, PAIRS) as i:
                        pe.wait_ge(sem("picked"), i + 1)
                        for n in range(2):
                            pe.wait_ge(sem("xt_taken"), i * 2 + (1 + n))
                            for j in range(4):
                                c = 4 * n + j
                                for a in range(TT):
                                    ins = nc.tensor.matmul(bank[4 + n][:, P * j:P * j + P], h_nat[:, a, P * c:P * c + P],
                                                           pick[:, a, :, :].rearrange("p e s -> p (e s)"), start=(a == 0), stop=(a == TT - 1))
                            ins.then_inc(sem("xt_ready"), 1)
                        for e2 in range(2):
                            rnd = rounds(i, e2)
                            quarters = ((0, 0, 0), (3, 64, 1), (1, 0, 1), (2, 64, 0))
                            pe.wait_ge(sem("h1_taken"), i * 2 + (1 + e2))
                            for q, at, b in quarters:
                                nc.tensor.matmul(bank[b][at:at + SLOTS, :], row_e[:, e2, :], b1_pad[:, 512 * q:512 * q + 512],
                                                 start=True, stop=False, skip_group_check=True)
                            if e2 == 0:
                                pe.wait_ge(sem("xt_taken"), i * 2 + 3)
                            for c in range(DC):
                                pe.wait_ge(loaded[c], rnd * 16 + 16)
                                for q, at, b in quarters:
                                    ins = nc.tensor.matmul(bank[b][at:at + SLOTS, :], xt[:, c, SLOTS * e2:SLOTS * e2 + SLOTS],
                                                           ring[:, c, 512 * q:512 * q + 512], start=False, stop=(c == DC - 1), skip_group_check=True)
                                ins.then_inc(used, 1)
                            if e2 == 0:
                                for a in range(TT):
                                    ins = nc.tensor.transpose(bank[7][:, P * a:P * a + P], pick_gate[:, a, :, :].rearrange("p e s -> p (e s)"), ident)
                                ins.then_inc(sem("gates_turned"), 1)
                            pe.wait_ge(sem("u_ready"), i * 2 + (e2 + 1))
                            for j in range(4):
                                ins = nc.tensor.transpose(bank[6][:, P * j:P * j + P], lin[:, P * j:P * j + P], ident)
                            ins.then_inc(sem("u_turned"), 1)
                            pe.wait_ge(sem("ut_ready"), i * 2 + (e2 + 1))
                            pe.wait_ge(sem("y_taken"), i * 4 + (1 + 2 * e2))
                            for k in range(4):
                                pe.wait_ge(loaded[8 + k], rnd * 16 + 16)
                                w = slot3(8 + k, 2)
                                for x in range(2):
                                    r = 2 * k + x
                                    for dh in range(2):
                                        ins = nc.tensor.matmul(bank[2 + dh][64 * dh:64 * dh + 64, :], ut[:, r % 4, 64 * (r // 4):64 * (r // 4) + 64],
                                                               w[:, x, 512 * dh:512 * dh + 512], start=(r == 0), stop=(r == 7))
                                ins.then_inc(used, 1)
                        pe.wait_ge(sem("y_taken"), i * 4 + 5)
                        pe.wait_ge(sem("gate_slots_ready"), i + 1)
                        for n in range(4):
                            b = bank[6 + n % 2]
                            if n >= 2:
                                pe.wait_ge(sem("acc_added"), i * 4 + (n - 1))
                            for j in range(2):
                                m = 2 * n + j
                                ins = nc.tensor.matmul(b[:, T * j:T * j + T], y[:, P * m:P * m + P], gate_slots[:, :], start=True, stop=True)
                            ins.then_inc(sem("back"), 1)

                @S.block.scalar
                def _(act):
                    act.sem_inc(sem("xt_taken"), 1)
                    act.sem_inc(sem("y_taken"), 1)
                    with act.Fori(0, PAIRS) as i:
                        for n in range(2):
                            act.wait_ge(sem("xt_ready"), i * 2 + (n + 1))
                            nc.scalar.activation(xt[:, 4 * n:4 * n + 4, :].rearrange("p c s -> p (c s)"), bank[4 + n][:, :], ACT.Copy).then_inc(sem("xt_taken"), 1)
                        for e2 in range(2):
                            act.wait_ge(sem("glu_ready"), i * 2 + (e2 + 1))
                            nc.scalar.activation(sg[:, :], glu[:, :], ACT.Sigmoid, scale=SW_ALPHA).then_inc(sem("sg_ready"), 1)
                            if e2 == 0:
                                act.wait_ge(sem("gates_turned"), i + 1)
                                nc.scalar.activation(gate_slots[:, :], bank[7][:, 0:T], ACT.Copy).then_inc(sem("gate_slots_ready"), 1)
                            act.wait_ge(sem("u_turned"), i * 2 + (e2 + 1))
                            nc.scalar.activation(ut[:, :, :].rearrange("p c s -> p (c s)"), bank[6][:, :], ACT.Copy).then_inc(sem("ut_ready"), 1)
                            act.wait_ge(used, rounds(i, e2) * RING + RING)
                            for dh in range(2):
                                nc.scalar.activation(y[64 * e2:64 * e2 + 64, 512 * dh:512 * dh + 512], bank[2 + dh][64 * dh:64 * dh + 64, :],
                                                     ACT.Copy).then_inc(sem("y_taken"), 1)

                @S.block.vector
                def _(dve):
                    def prepare(i):
                        for e2 in range(2):
                            for a in range(TT):
                                e = i * 2 + e2
                                nc.vector.tensor_scalar(pick[:, a, e2, :], const("slot"), rank[:, a, bass.ds(e, 1)], None, ALU.is_equal)
                                nc.vector.tensor_scalar(pick_gate[:, a, e2, :], const("slot"), rank[:, a, bass.ds(e, 1)],
                                                        gates[:, a, bass.ds(e, 1)], ALU.is_equal, ALU.mult)
                            ins = nc.vector.tensor_copy(row_e[:, e2, :], ident[:, bass.ds(i * 2 + e2, 1)].to_broadcast([P, SLOTS]))
                        ins.then_inc(sem("picked"), 1)

                    dve.sem_inc(sem("h1_taken"), 1)
                    with dve.Fori(0, PAIRS) as i:
                        dve.wait_ge(sem("back"), i * 4 + 1)
                        prepare(i)
                        for e2 in range(2):
                            dve.wait_ge(used, rounds(i, e2) * RING + 8)
                            for b in range(2):
                                pairs = bank[b][:, :].rearrange("p (f two) -> p f two", two=2)
                                nc.vector.tensor_scalar(lin[:, 256 * b:256 * b + 256], pairs[:, :, 1], LIMIT, -LIMIT, ALU.min, ALU.max)
                                ins = nc.vector.tensor_scalar(glu[:, 256 * b:256 * b + 256], pairs[:, :, 0], LIMIT, None, ALU.min)
                            ins.then_inc(sem("glu_ready"), 1)
                            dve.wait_ge(sem("glu_ready"), i * 2 + (e2 + 1))
                            nc.vector.scalar_tensor_tensor(lin[:, :], lin[:, :], 1.0, glu[:, :], ALU.add, ALU.mult).then_inc(sem("h1_taken"), 1)
                            dve.wait_ge(sem("h1_taken"), i * 2 + (e2 + 2))
                            dve.wait_ge(sem("sg_ready"), i * 2 + (e2 + 1))
                            nc.vector.tensor_tensor(lin[:, :], lin[:, :], sg[:, :], ALU.mult).then_inc(sem("u_ready"), 1)
                        for n in range(4):
                            dve.wait_ge(sem("back"), i * 4 + (n + 2))
                            av = flat(acc[:, 2 * n:2 * n + 2, :])
                            nc.vector.tensor_tensor(av, bank[6 + n % 2][:, :], av, ALU.add).then_inc(sem("acc_added"), 1)
                    dve.wait_ge(sem("acc_added"), 4 * PAIRS)
                    nc.vector.tensor_scalar(flat(rank[:, :, :]), flat(rank[:, :, :]), float(SLOTS), None, ALU.subtract)
        if stop == "experts":
            return
        moe.close()


        rope2 = sb("rope2", [P, 2, T])
        lower = sb("lower", [P, 2, 4])
        fox_bias = sb("fox_bias", [4, LAYERS])
        level_masks = sb("level_masks", [P, NLEV, P], U8)

        U_MIX = FFN_UNITS
        U_OUT = U_MIX + MIX_UNITS
        U_FFN2 = U_OUT + WOUT_UNITS
        MIX_COLS = {"hf": (2052, 2308), "hg": (3076, 3332), "hq": (1540, 1796), "hi": (2564, 2820),
                    "dq": (772,), "dk": (1028,), "fq": (0,), "fk": (256,), "fv": (512,), "dv": (1284,)}
        MIX_ORDER = [(name, j, at) for name, ats in MIX_COLS.items() for j, at in enumerate(ats)]
        assert len(MIX_ORDER) == MIX_UNITS

        def ffn_unit(n):
            if n < 2:
                return ("gate", "up")[n], 0
            if n == FFN_UNITS - 1:
                return "down", FT // 2 - 1
            g, k = divmod(n - 2, 3)
            return (("gate", g + 1), ("up", g + 1), ("down", g))[k]

        def load2(sp, L, n):
            if n >= RING:
                sp.wait_ge(used2, n - RING + 1)
            dst = ring[:, n % RING, :]
            if n < FFN_UNITS or n >= U_FFN2:
                which = "ffn1" if n < FFN_UNITS else "ffn2"
                mat, g = ffn_unit(n if n < FFN_UNITS else n - U_FFN2)
                w = A[f"{which}_w_{mat}_2"]
                if mat == "down":
                    dst = dst.rearrange("p (x n) -> p x n", x=2)
                    src = w[L, T * g:T * g + T, :].rearrange("(x p) n -> p x n", p=P)
                else:
                    dst = dst.rearrange("p (c n) -> p c n", c=DC)
                    src = w[L, :, T * g:T * g + T].rearrange("(c p) n -> p c n", p=P)
            else:
                dst = dst.rearrange("p (c n) -> p c n", c=DC)
                w, at = (A["w_in_2"], MIX_ORDER[n - U_MIX][2]) if n < U_OUT else (A["w_out_2"], T * (n - U_OUT))
                src = w[L, :, at:at + T].rearrange("(c p) n -> p c n", p=P)
            sp.dma_start(dst, src).then_inc(loaded2[n % RING], 16)

        def ready2(pe, n):
            pe.wait_ge(loaded2[n % RING], 16 * (n // RING + 1))

        with ExitStack() as c9, Stage(nc, pool) as S:
            sem = S.sem
            sq = sb("sq", [P, DC, T], where=c9)
            root = sb("root", [P, T], where=c9)
            posi = sb("posi", [P, T], I32, where=c9)
            posf = sb("posf", [P, T], where=c9)
            ang = sb("ang", [P, 2, T], where=c9)
            soft = sb("soft", [P, 4, 4], where=c9)
            levels = sb("levels", [P, NLEV * P], where=c9)
            ln_pe, ln_act, ln_dve = layer_norm(S, xT, "ln2_g", "ln2_b", root[:, :], sq, (0, 1))

            @S.block.tensor
            def _(pe):
                ln_pe(pe)

            @S.block.scalar
            def _(act):
                act.dma_start(posi[:, :], A["positions_2"].to_broadcast([P, T])).then_inc(sem("small"), 16)
                act.dma_start(fox_bias[:, :], A["fox_forget_bias_2"].rearrange("l h -> h l"), allow_slow_non_contiguous=True).then_inc(sem("small"), 16)
                act.dma_start(levels[:, :], A["const_levels"]).then_inc(sem("small"), 16)
                for j in range(2):
                    nc.scalar.activation(xT[:, 4 * j:4 * j + 4, :], xT[:, 4 * j:4 * j + 4, :], ACT.Copy, scale=ALPHA).then_inc(sem("x_scaled"), 1)
                ln_act(act)
                act.wait_ge(sem("angles_ready"), 1)
                nc.scalar.activation(rope2[:, :, :], rope2[:, :, :], ACT.Sin)
                act.wait_ge(sem("bounds_shifted"), 1)
                nc.scalar.activation(soft[:, 0:2, :], soft[:, 0:2, :], ACT.Exp).then_inc(sem("bounds_exp"), 1)

            @S.block.vector
            def _(dve):
                st = Steps(dve, sem, "dve_step")
                for m in range(DC):
                    dve.wait_ge(sem("x_scaled"), m // 4 + 1)
                    st.tell(nc.vector.scalar_tensor_tensor(xT[:, m, :], acc[:, m, :], mod[:, 40 + m:41 + m], xT[:, m, :],
                                                           ALU.mult, ALU.add), "x_ready")
                dve.wait_ge(sem("x_ready"), DC)
                ln_dve(dve, st)
                dve.wait_ge(sem("small"), 48)
                nc.vector.tensor_copy(flat(level_masks[:, :, :]), levels[:, :])
                st.step(nc.vector.tensor_copy(posf[:, :], posi[:, :]))
                rope_tables(dve, st, posf[:, :], const("freq_dil"), ang[:, 0, :], ang[:, 1, :], rope2[:, 0, :], rope2[:, 1, :])
                raw = par("hgrn_lower_bounds_2", 0, 8).rearrange("p (l c) -> p l c", l=LAYERS)
                st.step(nc.vector.tensor_tensor(soft[:, 2, :], raw[:, 0, :], raw[:, 1, :], ALU.max))
                st.step(nc.vector.tensor_tensor(soft[:, 0:2, :], raw, soft[:, 2:3, :].to_broadcast([P, 2, 4]), ALU.subtract), "bounds_shifted")
                dve.wait_ge(sem("bounds_exp"), 1)
                st.step(nc.vector.tensor_tensor(soft[:, 2, :], soft[:, 0, :], soft[:, 1, :], ALU.add))
                st.step(nc.vector.reciprocal(soft[:, 2, :], soft[:, 2, :]))
                st.step(nc.vector.tensor_tensor(soft[:, 0:2, :], soft[:, 0:2, :], soft[:, 2:3, :].to_broadcast([P, 2, 4]), ALU.mult))
                st.step(nc.vector.tensor_tensor(soft[:, 3, :], soft[:, 0, :], soft[:, 1, :], ALU.add))
                st.step(nc.vector.tensor_tensor(lower[:, 0, :], soft[:, 0, :], soft[:, 0, :], ALU.subtract))
                st.step(nc.vector.tensor_tensor(lower[:, 1, :], soft[:, 3, :], soft[:, 0, :], ALU.subtract))
                st.step(nc.vector.tensor_scalar(lower[:, :, :], lower[:, :, :], 0.0, 1.0 - 1e-6, ALU.max, ALU.min))
        if stop == "post_moe":
            return

        def split_high(act, sem, split, base_unit, r, n):
            u, bufs = base_unit + n, split[0].shape[1]
            act.wait_ge(loaded2[u % RING], r * 16 + 16 * (u // RING + 1))
            if n >= bufs:
                act.wait_ge(used2, r * RING + (u - bufs + 1))
            nc.scalar.activation(split[0][:, n % bufs, :], ring[:, u % RING, :], ACT.Copy).then_inc(sem("high_ready"), 1)

        def split_low(dve, sem, split, base_unit, r, n):
            bufs = split[0].shape[1]
            dve.wait_ge(sem("high_ready"), r * RING + (n + 1))
            nc.vector.tensor_tensor(split[1][:, n % bufs, :], ring[:, (base_unit + n) % RING, :], split[0][:, n % bufs, :].bitcast(F32),
                                    ALU.subtract).then_inc(sem("low_ready"), 1)

        def rms_norm(S, x, h, gain, root, sq, b, before_root=(), h_parts=None):
            sem = S.sem
            h_high, h_low = h_parts or (None, None)
            total = bank[b][:, 0:T]

            def tensor(pe):
                for c in range(DC):
                    if c % 4 == 0:
                        pe.wait_ge(sem("squares"), c // 4 + 1)
                    ins = nc.tensor.matmul(total, ones, sq[:, c, :], start=(c == 0), stop=(c == DC - 1))
                ins.then_inc(sem("total_ready"), 1)

            def scalar(act):
                for j in range(2):
                    nc.scalar.activation(sq[:, 4 * j:4 * j + 4, :], x[:, 4 * j:4 * j + 4, :], ACT.Square).then_inc(sem("squares"), 1)
                if before_root:
                    before_root[0](act)
                act.wait_ge(sem("total_ready"), 1)
                nc.scalar.activation(root, total, ACT.Sqrt, bias=1e-6, scale=1.0 / D).then_inc(sem("root_ready"), 1)
                if h_high is not None:
                    for c in range(DC):
                        act.wait_ge(sem("h_made"), c + 1)
                        nc.scalar.activation(h_high[:, c, :], h[:, c, :], ACT.Copy).then_inc(sem("h_high_ready"), 1)

            def vector(dve, st):
                if before_root:
                    before_root[1](dve)
                dve.wait_ge(sem("root_ready"), 1)
                st.step(nc.vector.reciprocal(root, root))

                def low(c):
                    dve.wait_ge(sem("h_high_ready"), c + 1)
                    st.tell(nc.vector.tensor_tensor(h_low[:, c, :], h[:, c, :], h_high[:, c, :].bitcast(F32), ALU.subtract), "h_ready")

                for c in range(DC):
                    st.tell(nc.vector.scalar_tensor_tensor(h[:, c, :], x[:, c, :], gain[:, c:c + 1], root, ALU.mult, ALU.mult),
                            "h_ready" if h_high is None else "h_made")
                for c in range(DC if h_parts else 0):
                    low(c)

            return tensor, scalar, vector

        def ffn_stage(L, base_unit, norm_name):
            with ExitStack() as cf, Stage(nc, pool) as S:
                sem = S.sem
                root = sb("root", [P, T], where=cf)
                gain = sb("gain", [P, DC], where=cf)
                silu = sb("silu", [P, 2, 512], where=cf)
                u_parts = [sb(f"u_{part}", [P, 2, 512], F32R, where=cf) for part in ("high", "low")]
                AHEAD = 2
                split = [sb(f"w_{part}", [P, AHEAD + 1, SLOT], F32R, where=cf) for part in ("high", "low")]
                h_parts = [sb(f"h_{part}", [P, DC, T], F32R, where=cf) for part in ("high", "low")]
                G = FT // 2
                LOOP_AT, REPS = 5, 2
                BODY = RING // 3
                kind = [ffn_unit(n) for n in range(FFN_UNITS)]
                unit = {k: n for n, k in enumerate(kind)}

                n_pe, n_act, n_dve = rms_norm(S, xT, hT, gain, root[:, :], hT, 0,
                                              (lambda act: split_high(act, sem, split, base_unit, 0, 0),
                                               lambda dve: split_low(dve, sem, split, base_unit, 0, 0)), h_parts)

                def used_up_to(r, mat, g):
                    return r * RING + (base_unit + unit[(mat, g)] + 1)

                @S.block.sync
                def _(sp):
                    for n in range(base_unit + RING if base_unit else 0, min(base_unit + FFN_UNITS + RING, LAYER_UNITS)):
                        load2(sp, L, n)

                @S.block.tensor
                def _(pe):
                    def multiply(r, n):
                        mat, g = kind[n]
                        if n:
                            pe.wait_ge(sem("low_ready"), r * RING + (n + 1))
                        else:
                            pe.wait_ge(sem("high_ready"), 1)
                        w_parts = [part[:, n % (AHEAD + 1), :] for part in split]
                        if mat == "down":
                            pe.wait_ge(sem("u_ready"), r * BODY + (g + 1))
                            passes = parts_of(w_parts, [part[:, g % 2, :] for part in u_parts])
                            order = [(k, x, m) for k in range(3) for x in range(2) for m in range(DC)]
                            if g == G - 1:
                                order.sort(key=lambda o: o[2] // 2)
                            for i, (k, x, m) in enumerate(order):
                                w, v = passes[k]
                                at = D * x + P * m
                                ins = nc.tensor.matmul(bank[4 + m // 2][:, T * (m % 2):T * (m % 2) + T], w[:, at:at + P], v[:, T * x:T * x + T],
                                                       start=(g == 0 and k == 0 and x == 0 and m % 2 == 0),
                                                       stop=(g == G - 1 and k == 2 and x == 1), skip_group_check=True)
                                if g == G - 1 and i % 12 == 11 and i < 47:
                                    ins.then_inc(sem("sum_ready"), 1)
                        else:
                            b = bank[2 * (g % 2) + (mat == "up")]
                            if g >= 2:
                                pe.wait_ge(sem("u_ready"), r * BODY + (g - 1))
                            passes = parts_of(w_parts, h_parts)
                            for k, (w, h) in enumerate(passes):
                                if n == 0 and k == 1:
                                    pe.wait_ge(sem("low_ready"), 1)
                                for x in range(2):
                                    for c in range(DC):
                                        if n == 0 and x == 0 and k != 1:
                                            pe.wait_ge(sem("h_ready" if k else "h_high_ready"), c + 1)
                                        at = T * c + P * x
                                        ins = nc.tensor.matmul(b[:, T * x:T * x + T], w[:, at:at + P], h[:, c, :],
                                                               start=(k == 0 and x == 0 and c == 0), stop=(k == 2 and c == DC - 1), skip_group_check=True)
                        ins.then_inc(used2, 1)

                    n_pe(pe)
                    for n in range(LOOP_AT):
                        multiply(0, n)
                    with pe.Fori(0, REPS) as r:
                        for n in range(LOOP_AT, LOOP_AT + RING):
                            multiply(r, n)
                    for n in range(LOOP_AT + REPS * RING, FFN_UNITS):
                        multiply(0, n)

                @S.block.scalar
                def _(act):
                    def during(r, n):
                        mat, g = kind[n - 1]
                        if n >= 1 and mat == "gate":
                            act.wait_ge(used2, used_up_to(r, "gate", g))
                            if g >= 2:
                                act.wait_ge(sem("u_ready"), r * BODY + (g - 1))
                            nc.scalar.activation(silu[:, g % 2, :], bank[2 * (g % 2)][:, :], ACT.Silu).then_inc(sem("silu_ready"), 1)
                        if n + AHEAD < FFN_UNITS:
                            split_high(act, sem, split, base_unit, r, n + AHEAD)

                    n_act(act)
                    split_high(act, sem, split, base_unit, 0, 1)
                    for n in range(LOOP_AT):
                        during(0, n)
                    with act.Fori(0, REPS) as r:
                        for n in range(LOOP_AT, LOOP_AT + RING):
                            during(r, n)
                    for n in range(LOOP_AT + REPS * RING, FFN_UNITS):
                        during(0, n)

                @S.block.vector
                def _(dve):
                    st = Steps(dve, sem, "dve_step")
                    st.step(nc.vector.tensor_copy(gain[:, :], params[:, bass.ds(L * DC + AT[norm_name], DC)]))

                    def during(r, n):
                        mat, g = kind[n - 1]
                        if n >= 1 and mat == "up":
                            dve.wait_ge(used2, used_up_to(r, "up", g))
                            dve.wait_ge(sem("silu_ready"), r * BODY + (g + 1))
                            if g >= 2:
                                dve.wait_ge(used2, used_up_to(r, "down", g - 2))
                            u, high, low = silu[:, g % 2, :], u_parts[0][:, g % 2, :], u_parts[1][:, g % 2, :]
                            nc.vector.tensor_tensor(u, u, bank[2 * (g % 2) + 1][:, :], ALU.mult).then_inc(sem("u_made"), 1)
                            dve.wait_ge(sem("u_made"), r * BODY + (g + 1))
                            nc.vector.tensor_copy(high, u).then_inc(sem("u_high_made"), 1)
                            dve.wait_ge(sem("u_high_made"), r * BODY + (g + 1))
                            nc.vector.tensor_tensor(low, u, high.bitcast(F32), ALU.subtract).then_inc(sem("u_ready"), 1)
                        if n + AHEAD < FFN_UNITS:
                            split_low(dve, sem, split, base_unit, r, n + AHEAD)

                    n_dve(dve, st)
                    split_low(dve, sem, split, base_unit, 0, 1)
                    for n in range(LOOP_AT):
                        during(0, n)
                    with dve.Fori(0, REPS) as r:
                        for n in range(LOOP_AT, LOOP_AT + RING):
                            during(r, n)
                    for n in range(LOOP_AT + REPS * RING, FFN_UNITS):
                        during(0, n)
                    for m in range(4):
                        if m < 3:
                            dve.wait_ge(sem("sum_ready"), m + 1)
                        else:
                            dve.wait_ge(used2, used_up_to(0, "down", G - 1))
                        xm = flat(xT[:, 2 * m:2 * m + 2, :])
                        nc.vector.scalar_tensor_tensor(xm, bank[4 + m][:, :], 0.5, xm, ALU.mult, ALU.add)

        def mixing_stages(L):
            with ExitStack() as cm:
                qk = sb("qk", [P, 8, T], where=cm)
                vv = sb("vv", [P, 2, TT, T], where=cm)
                qp = sb("qp", [P, 4, T], where=cm)
                kr = sb("kr", [P, 4, T], where=cm)
                fgt = sb("fgt", [P, 4, T], where=cm)
                hv = sb("hv", [P, TT, 512], where=cm)
                hg = sb("hg", [P, 4, T], where=cm)
                fox_c = sb("fox_c", [P, T], where=cm)
                tile_of = {"fq": 0, "fk": 2, "dq": 4, "dk": 6}

                with ExitStack() as c, Stage(nc, pool) as S:
                    sem = S.sem
                    root = qk[:, 0, :]
                    gain = sb("gain", [P, DC], where=c)
                    w_ff = sb("w_ff", [P, DC, 4], where=c)
                    one_less = sb("one_less", [P, 4], where=c)
                    floor = sb("floor", [P, 4], where=c)
                    keep = sb("keep", [P, 4], where=c)
                    fz = hT[0:4, 0:3, :]
                    AHEAD = 1
                    ff_parts = [sb(f"ff_{part}", [P, DC, 4], F32R, where=c) for part in ("high", "low")]
                    split = [sb(f"w_{part}", [P, AHEAD + 1, SLOT], F32R, where=c) for part in ("high", "low")]
                    h_parts = [sb(f"h_{part}", [P, DC, T], F32R, where=c) for part in ("high", "low")]

                    n_pe, n_act, n_dve = rms_norm(S, xT, hT, gain, root, hT, 0,
                                                  (lambda act: split_high(act, sem, split, U_MIX, 0, 0),
                                                   lambda dve: split_low(dve, sem, split, U_MIX, 0, 0)), h_parts)
                    on_act = [n for n, (name, _, _) in enumerate(MIX_ORDER) if name in ("hf", "hg", "hq", "fv", "dv")]
                    on_dve = [n for n in range(MIX_UNITS) if n not in on_act]
                    taken_by = lambda n: ("act_took", on_act.index(n) + 1) if n in on_act else ("dve_took", on_dve.index(n) + 1)

                    @S.block.sync
                    def _(sp):
                        sp.dma_start(w_ff[:, :, :], A["w_in_2"][L, :, 768:772].rearrange("(c p) n -> p c n", p=P)).then_inc(sem("ff_loaded"), 16)
                        for n in range(U_MIX + RING, U_OUT + RING):
                            load2(sp, L, n)

                    @S.block.tensor
                    def _(pe):
                        n_pe(pe)
                        for n, (name, j, _) in enumerate(MIX_ORDER):
                            pe.wait_ge(sem("low_ready" if n else "high_ready"), n + 1)
                            b = bank[(n + 1) % 7]
                            if n >= 7:
                                pe.wait_ge(sem(taken_by(n - 7)[0]), taken_by(n - 7)[1])
                            passes = parts_of([part[:, n % (AHEAD + 1), :] for part in split], h_parts)
                            for k, (w, h) in enumerate(passes):
                                if n == 0 and k == 1:
                                    pe.wait_ge(sem("low_ready"), 1)
                                for x in range(2):
                                    for c_ in range(DC):
                                        if n == 0 and x == 0 and k != 1:
                                            pe.wait_ge(sem("h_ready" if k else "h_high_ready"), c_ + 1)
                                        flags = dict(start=(k == 0 and x == 0 and c_ == 0), stop=(k == 2 and c_ == DC - 1), skip_group_check=True)
                                        if name in ("fv", "dv", "hi"):
                                            ins = nc.tensor.matmul(b[:, T * x:T * x + T], h[:, c_, P * x:P * x + P], w[:, T * c_:T * c_ + T], **flags)
                                        else:
                                            at = T * c_ + P * x
                                            ins = nc.tensor.matmul(b[:, T * x:T * x + T], w[:, at:at + P], h[:, c_, :], **flags)
                            ins.then_inc(used2, 1)
                            if n == 0:
                                pe.wait_ge(sem("ff_low_ready"), 1)
                                for k, (w, h) in enumerate(parts_of(ff_parts, h_parts)):
                                    for c_ in range(DC):
                                        ins = nc.tensor.matmul(bank[7][0:4, 0:T], w[:, c_, :], h[:, c_, :], start=(k == 0 and c_ == 0), stop=(k == 2 and c_ == DC - 1))
                                ins.then_inc(sem("ff_ready"), 1)

                    @S.block.scalar
                    def _(act):
                        st = Steps(act, sem, "act_step")
                        n_act(act)

                        def take(n):
                            name, j, _ = MIX_ORDER[n]
                            act.wait_ge(used2, U_MIX + n + 1)
                            b = bank[(n + 1) % 7][:, :]
                            two = slice(2 * j, 2 * j + 2)
                            if name == "hf":
                                nc.scalar.activation(flat(fgt[:, two, :]), b, ACT.Sigmoid).then_inc(sem("sig_ready"), 1)
                                ins = nc.scalar.activation(flat(kr[:, two, :]), b, ACT.Sigmoid, scale=-1.0)
                            elif name == "hg":
                                ins = nc.scalar.activation(flat(hg[:, two, :]), b, ACT.Sigmoid)
                            elif name == "hq":
                                ins = nc.scalar.activation(flat(qp[:, two, :]), b, ACT.Silu)
                            else:
                                ins = nc.scalar.activation(vv[:, 0 if name == "fv" else 1, :, :].rearrange("p a n -> p (a n)"), b, ACT.Copy)
                            ins.then_inc(sem("act_took"), 1)

                        for n in range(MIX_UNITS + 1):
                            if n - 1 in on_act:
                                take(n - 1)
                            if n + AHEAD < MIX_UNITS:
                                split_high(act, sem, split, U_MIX, 0, n + AHEAD)
                        act.wait_ge(sem("minus_abs"), 1)
                        st.step(nc.scalar.activation(fz[:, 1, :], fz[:, 1, :], ACT.Exp))
                        st.tell(nc.scalar.activation(fz[:, 1, :], fz[:, 1, :], ACT.Ln, bias=1.0), "log_ready")

                    @S.block.vector
                    def _(dve):
                        st = Steps(dve, sem, "dve_step")
                        st.step(nc.vector.tensor_copy(gain[:, :], params[:, bass.ds(L * DC + AT["mix_norm_2"], DC)]))
                        st.step(nc.vector.tensor_copy(keep[:, :], lower[:, bass.ds(L, 1), :].rearrange("p a c -> p (a c)")))
                        nc.vector.tensor_scalar(one_less[:, :], keep[:, :], -1.0, 1.0, ALU.mult, ALU.add)
                        st.step(nc.vector.tensor_scalar(floor[:, :], keep[:, :], LB_FLOOR, None, ALU.max))
                        dve.wait_ge(sem("ff_loaded"), 16)
                        st.step(nc.vector.tensor_copy(ff_parts[0][:, :, :], w_ff[:, :, :]))
                        st.tell(nc.vector.tensor_tensor(ff_parts[1][:, :, :], w_ff[:, :, :], ff_parts[0][:, :, :].bitcast(F32), ALU.subtract), "ff_low_ready")
                        n_dve(dve, st)
                        nc.vector.memset(fox_c[:, :], 0.0)

                        def forget_logits():
                            dve.wait_ge(sem("ff_ready"), 1)
                            st.step(nc.vector.tensor_scalar(fz[:, 0, :], bank[7][0:4, 0:T], fox_bias[:, bass.ds(L, 1)], None, ALU.add))
                            st.tell(nc.vector.scalar_tensor_tensor(fz[:, 1, :], fz[:, 0, :], -1.0, fz[:, 0, :], ALU.mult, ALU.min), "minus_abs")

                        def bounds(j):
                            dve.wait_ge(sem("act_took"), j + 1)
                            for h in (2 * j, 2 * j + 1):
                                nc.vector.tensor_scalar(fgt[:, h, :], fgt[:, h, :], one_less[:, h:h + 1], floor[:, h:h + 1], ALU.mult, ALU.add)
                                nc.vector.tensor_scalar(kr[:, h, :], kr[:, h, :], one_less[:, h:h + 1], None, ALU.mult)

                        def take(n):
                            name, j, _ = MIX_ORDER[n]
                            dve.wait_ge(used2, U_MIX + n + 1)
                            b = bank[(n + 1) % 7][:, :]
                            if name == "hi":
                                ins = nc.vector.tensor_copy(hv[:, :, T * j:T * j + T], b.rearrange("p (a n) -> p a n", a=2))
                            else:
                                t0 = tile_of[name]
                                ins = nc.vector.tensor_copy(flat(qk[:, t0:t0 + 2, :]), b)
                            st.tell(ins, "dve_took")

                        for n in range(MIX_UNITS + 1):
                            if n - 1 in on_dve:
                                take(n - 1)
                            if n + AHEAD < MIX_UNITS:
                                split_low(dve, sem, split, U_MIX, 0, n + AHEAD)
                            if n == 1:
                                forget_logits()
                            elif n in (2, 3):
                                bounds(n - 2)
                        dve.wait_ge(sem("log_ready"), 1)
                        st.step(nc.vector.scalar_tensor_tensor(fz[:, 0, :], fz[:, 0, :], 0.0, fz[:, 1, :], ALU.min, ALU.subtract))
                        nc.vector.memset(fz[:, 2, :], 1.0)
                        st.step(nc.vector.memset(fz[:, 1, 0:1], 0.0))
                        st.step(nc.vector.tensor_tensor_scan(fz[:, 1, :], fz[:, 2, :], fz[:, 0, :], 0.0, ALU.mult, ALU.add))
                        st.step(nc.vector.tensor_scalar(fox_c[0:4, :], fz[:, 1, :], -8.0, None, ALU.mult))
                if stop == "mix_proj":
                    return

                with ExitStack() as c, Stage(nc, pool) as S:
                    sem = S.sem
                    tmp = sb("tmp", [P, 4, T], where=c)
                    attention_buffers(S, c)
                    causal = const("causal").rearrange("p (a k) -> p a k", a=TT)
                    dilated = const("dilated").rearrange("p (a k) -> p a k", a=TT)
                    pick_head = const("pick_head").rearrange("p (h t) -> p h t", h=4)
                    att_pe, att_dve, att_act = attention(8, 0.125)
                    at_ = sb("at", [P, 4, 3, P], where=c)
                    prods = sb("prods", [P, 4 * T], where=c)
                    sq = sb("sq", [P, 4, T], where=c)
                    onorm = sb("onorm", [P, 4], where=c)
                    o = hT[:, 4:8, :]

                    @S.block.gpsimd
                    def _(gps):
                        nc.gpsimd.memset(at_[:, :, :, :], 0.0).then_inc(sem("cleared"), 1)

                    @S.block.tensor
                    def _(pe):
                        for j in range(2):
                            nc.tensor.matmul(bank[6 + j][:, :], const("rot_dil"), flat(qk[:, 4 + 2 * j:6 + 2 * j, :]), start=True, stop=True
                                             ).then_inc(sem("partners"), 1)

                        def scores(h, a):
                            rows = slice(64 * (h % 2), 64 * (h % 2) + 64)
                            t0 = (0 if h < 4 else 4) + h // 2 % 2
                            parts = [(qk[rows, t0, P * a:P * a + P], qk[rows, t0 + 2, :])]
                            if h < 4:
                                parts.append((pick_head[:, h, :], fox_c[:, :]))
                            return parts

                        def level(n):
                            if n >= NLEV:
                                return
                            if n == 0:
                                pe.wait_ge(sem("rotated"), 1)
                            else:
                                pe.wait_ge(sem("factors"), n)
                            for h in range(4):
                                if n and h % 2 == 0:
                                    pe.wait_ge(sem("masked_in"), 2 * (n - 1) + h // 2 + 1)
                                for a in range(TT):
                                    at = P * (2 * (h % 2) + a)
                                    ins = nc.tensor.matmul(bank[6 + h // 2][:, at:at + P], kr[:, h, P * a:P * a + P], qp[:, h, P * a:P * a + P],
                                                           start=True, stop=True)
                                if h % 2:
                                    ins.then_inc(sem("level_ready"), 1)

                        att_pe(pe, S, scores, lambda h, a: vv[:, h // 4, a, 64 * (h % 4):64 * (h % 4) + 64], level)
                        pe.wait_ge(sem("factors"), NLEV)
                        pe.wait_ge(sem("masked_in"), 2 * NLEV)
                        for h in range(4):
                            ins = nc.tensor.matmul(bank[6][:, P * h:P * h + P], kr[:, h, 0:P], qp[:, h, P:T], start=True, stop=True)
                        ins.then_inc(sem("level_ready"), 1)
                        pe.wait_ge(sem("at_ready"), 1)
                        for h in range(4):
                            b = bank[7 - h // 2][:, T * (h % 2):T * (h % 2) + T]
                            nc.tensor.matmul(b, hv[:, 0, P * h:P * h + P], at_[:, h, 0:2, :].rearrange("p a t -> p (a t)"),
                                             start=True, stop=False, skip_group_check=True)
                            ins = nc.tensor.matmul(b[:, P:T], hv[:, 1, P * h:P * h + P], at_[:, h, 2, :], start=False, stop=True, skip_group_check=True)
                            if h % 2:
                                ins.then_inc(sem("o_ready"), 1)
                        for j in range(2):
                            pe.wait_ge(sem("o_squares"), j + 1)
                            nc.tensor.matmul(bank[j][:, :], ones, flat(sq[:, 2 * j:2 * j + 2, :]), start=True, stop=True).then_inc(sem("o_sums"), 1)

                    @S.block.scalar
                    def _(act):
                        att_act(act, Steps(act, sem, "act_step"), S)
                        for j in range(2):
                            act.wait_ge(sem("o_ready"), j + 1)
                            nc.scalar.activation(flat(sq[:, 2 * j:2 * j + 2, :]), bank[7 - j][:, :], ACT.Square).then_inc(sem("o_squares"), 1)
                            nc.scalar.activation(flat(o[:, 2 * j:2 * j + 2, :]), bank[7 - j][:, :], ACT.Copy).then_inc(sem("o_taken"), 1)
                        for j in range(2):
                            act.wait_ge(sem("o_sums"), j + 1)
                            nc.scalar.activation(flat(sq[:, 2 * j:2 * j + 2, :]), bank[j][:, :], ACT.Sqrt, bias=1e-6, scale=1.0 / P).then_inc(sem("o_roots"), 1)

                    @S.block.vector
                    def _(dve):
                        st = Steps(dve, sem, "dve_step")
                        cos2 = rope2[:, 0:1, :].to_broadcast([P, 2, T])
                        sin2 = rope2[:, 1:2, :].to_broadcast([P, 2, T])
                        dve.wait_ge(sem("partners"), 2)
                        for j in range(2):
                            q = qk[:, 4 + 2 * j:6 + 2 * j, :]
                            st.step(nc.vector.tensor_tensor(q, q, cos2, ALU.mult))
                            st.step(nc.vector.tensor_tensor(tmp[:, 2 * j:2 * j + 2, :], bank[6 + j][:, :].rearrange("p (a t) -> p a t", a=2), sin2, ALU.mult))
                        st.step(nc.vector.tensor_tensor(qk[:, 4:8, :], qk[:, 4:8, :], tmp[:, :, :], ALU.add), "rotated")
                        st.step(nc.vector.tensor_copy(onorm[:, :], params[:, bass.ds(L * 4 + AT["hgrn_out_norm_2"], 4)]))
                        joined = [fgt[:, :, :].rearrange("p h t -> p (h t)")]
                        free = [0]

                        def level(n):
                            if n >= NLEV:
                                return
                            dve.wait_ge(sem("level_ready"), 2 * n + 2)
                            q_, k_, prev = flat(qp[:, :, :]), flat(kr[:, :, :]), joined[-1]
                            if n == 0:
                                st.tell(nc.vector.tensor_tensor(q_, q_, prev, ALU.mult), "factors")
                            else:
                                b = 2 ** (n - 1)
                                q4 = q_.rearrange("p (k two b) -> p k two b", two=2, b=b)
                                k4 = k_.rearrange("p (k two b) -> p k two b", two=2, b=b)
                                halves = prev.rearrange("p (k two) -> p k two", two=2)
                                blocks = 4 * T // (2 * b)
                                nc.vector.tensor_tensor(q4[:, :, 1, :], q4[:, :, 1, :], halves[:, :, 0:1].to_broadcast([P, blocks, b]), ALU.mult)
                                new = prods[:, free[0]:free[0] + blocks]
                                nc.vector.tensor_tensor(new, halves[:, :, 0], halves[:, :, 1], ALU.mult)
                                free[0] += blocks
                                joined.append(new)
                                st.tell(nc.vector.tensor_tensor(k4[:, :, 0, :], k4[:, :, 0, :], halves[:, :, 1:2].to_broadcast([P, blocks, b]), ALU.mult), "factors")
                            if n == 0:
                                dve.wait_ge(sem("cleared"), 1)
                            for j in range(2):
                                blocks = at_[:, 2 * j:2 * j + 2, :, :].rearrange("p h b t -> p (h b) t")
                                for h in range(2):
                                    ins = nc.vector.copy_predicated(blocks[:, 3 * h:3 * h + 3:2, :],
                                                                    level_masks[:, n:n + 1, :].to_broadcast([P, 2, P]),
                                                                    bank[6 + j][:, T * h:T * h + T].rearrange("p (a t) -> p a t", a=2))
                                st.step(ins, "masked_in")

                        att_dve(dve, st, S, lambda h: causal if h < 4 else dilated, lambda pair: hT[:, pair, :], level)
                        dve.wait_ge(sem("level_ready"), 2 * NLEV + 1)
                        st.step(nc.vector.tensor_copy(at_[:, :, 1, :], bank[6][:, :].rearrange("p (h t) -> p h t", h=4)), "at_ready")
                        for j in range(2):
                            oj, sj = flat(o[:, 2 * j:2 * j + 2, :]), flat(sq[:, 2 * j:2 * j + 2, :])
                            dve.wait_ge(sem("o_roots"), j + 1)
                            dve.wait_ge(sem("o_taken"), j + 1)
                            st.step(nc.vector.reciprocal(sj, sj))
                            st.step(nc.vector.tensor_tensor(oj, oj, sj, ALU.mult))
                            for h in (2 * j, 2 * j + 1):
                                st.step(nc.vector.scalar_tensor_tensor(o[:, h, :], o[:, h, :], onorm[:, h:h + 1], hg[:, h, :], ALU.mult, ALU.mult))
                if stop in ("mix_att", "mix_hgrn"):
                    return

            with ExitStack() as c, Stage(nc, pool) as S:
                sem = S.sem
                split = [sb(f"w_{part}", [P, 3, SLOT], F32R, where=c) for part in ("high", "low")]
                mix_parts = [sb(f"mix_{part}", [P, DC, T], F32R, where=c) for part in ("high", "low")]

                @S.block.sync
                def _(sp):
                    for n in range(U_OUT + RING, U_FFN2 + RING):
                        load2(sp, L, n)

                @S.block.tensor
                def _(pe):
                    for n in range(WOUT_UNITS):
                        pe.wait_ge(sem("low_ready" if n else "high_ready"), n + 1)
                        for k, (w, h) in enumerate(parts_of([part[:, n % 3, :] for part in split], mix_parts)):
                            if n == 0:
                                pe.wait_ge(sem(("mix_high_ready", "low_ready", "mix_low_ready")[k]), 1)
                            for x in range(2):
                                for c_ in range(DC):
                                    at = T * c_ + P * x
                                    ins = nc.tensor.matmul(bank[n][:, T * x:T * x + T], w[:, at:at + P], h[:, c_, :],
                                                           start=(k == 0 and x == 0 and c_ == 0), stop=(k == 2 and c_ == DC - 1), skip_group_check=True)
                        ins.then_inc(used2, 1)

                @S.block.scalar
                def _(act):
                    split_high(act, sem, split, U_OUT, 0, 0)
                    nc.scalar.activation(mix_parts[0][:, :, :], hT[:, :, :], ACT.Copy).then_inc(sem("mix_high_ready"), 1)
                    for n in range(1, WOUT_UNITS):
                        split_high(act, sem, split, U_OUT, 0, n)

                @S.block.vector
                def _(dve):
                    split_low(dve, sem, split, U_OUT, 0, 0)
                    dve.wait_ge(sem("mix_high_ready"), 1)
                    nc.vector.tensor_tensor(mix_parts[1][:, :, :], hT[:, :, :], mix_parts[0][:, :, :].bitcast(F32), ALU.subtract
                                            ).then_inc(sem("mix_low_ready"), 1)
                    for n in range(1, WOUT_UNITS):
                        split_low(dve, sem, split, U_OUT, 0, n)
                    for n in range(WOUT_UNITS):
                        dve.wait_ge(used2, U_OUT + n + 1)
                        xm = flat(xT[:, 2 * n:2 * n + 2, :])
                        nc.vector.tensor_tensor(xm, bank[n][:, :], xm, ALU.add)

        with nc.Fori(0, LAYERS) as L:
            ffn_stage(L, 0, "ffn1_norm_2")
            if stop == "ffn1":
                return
            mixing_stages(L)
            if stop and stop.startswith("mix"):
                return
            ffn_stage(L, U_FFN2, "ffn2_norm_2")
            nc.all_engine_barrier(sems_to_clear=range(loaded2[0].num, used2.num + 1))

        with ExitStack() as ce, Stage(nc, pool) as S:
            sem = S.sem
            sq = sb("sq", [P, DC, T], where=ce)
            root = sb("root", [P, T], where=ce)
            y = sb("y_out", [P, TT, D], where=ce)
            n_pe, n_act, n_dve = rms_norm(S, xT, hT, par("final_norm_2", 0, 8), root[:, :], sq, 0)
            out_rows = out[0].rearrange("(a p) d -> p a d", p=P)

            @S.block.tensor
            def _(pe):
                n_pe(pe)
                for n in range(4):
                    for j in range(4):
                        c = 4 * (n // 2) + j
                        pe.wait_ge(sem("h_ready"), c + 1)
                        ins = nc.tensor.transpose(bank[1 + n][:, P * j:P * j + P], hT[:, c, P * (n % 2):P * (n % 2) + P], ident)
                    ins.then_inc(sem("y_turned"), 1)

            @S.block.scalar
            def _(act):
                n_act(act)
                for n in range(4):
                    act.wait_ge(sem("y_turned"), n + 1)
                    nc.scalar.activation(y[:, n % 2, 512 * (n // 2):512 * (n // 2) + 512], bank[1 + n][:, :], ACT.Copy).then_inc(sem("y_ready"), 1)

            @S.block.vector
            def _(dve):
                n_dve(dve, Steps(dve, sem, "dve_step"))

            @S.block.sync
            def _(sp):
                for n in range(4):
                    sp.wait_ge(sem("y_ready"), n + 1)
                    cols = slice(512 * (n // 2), 512 * (n // 2) + 512)
                    sp.dma_start(out_rows[:, n % 2, cols], y[:, n % 2, cols]).then_inc(sem("stored"), 16)
                sp.wait_ge(sem("stored"), 64)


INPUTS = ["x", "c", "positions", "emb_ln_g", "emb_ln_b", "ada_w", "ada_b", "w_in", "q_norm_g", "w_uq", "kv_norm_g",
          "w_uk", "w_uv", "mla_out_g", "rwkv_mu", "rwkv_w0", "rwkv_w2", "rwkv_a0", "rwkv_a2", "rwkv_g2", "rwkv_k_k",
          "rwkv_k_a", "rwkv_r_k", "rwkv_gn_g", "rwkv_gn_b", "w_o", "ln1_g", "ln1_b", "router_w", "router_b", "exp_w1",
          "exp_b1", "exp_w2", "exp_b2", "ln2_g", "ln2_b", "positions_2", "ffn1_norm_2", "ffn1_w_gate_2",
          "ffn1_w_up_2", "ffn1_w_down_2", "mix_norm_2", "w_in_2", "fox_forget_bias_2", "hgrn_lower_bounds_2",
          "hgrn_out_norm_2", "w_out_2", "ffn2_norm_2", "ffn2_w_gate_2", "ffn2_w_up_2", "ffn2_w_down_2", "final_norm_2"]


def flat_rows(a):
    n = len(a.shape)
    if n == 1:
        return a.rearrange("(r k) -> r k", k=P)
    if n == 2:
        return a.rearrange("l (r k) -> (l r) k", k=P)
    return a.rearrange("l (r h) k -> (l r) (h k)", h=2)


def side_by_side(parts):
    return np.concatenate([np.asarray(a, np.float32) for a in parts.values()], 1)


def kernel(**inputs):
    import concourse.bacc as bacc
    from concourse.bass_utils import run_bass_kernel_spmd as run

    nc = bacc.Bacc("TRN2", target_bir_lowering=False, num_devices=1)
    arrays = {name: np.ascontiguousarray(inputs[name]) for name in INPUTS}
    arrays["const_base"] = side_by_side(BASE_PARTS)
    arrays["const_rwkv"] = side_by_side(RWKV_PARTS)
    arrays["const_levels"] = LEVEL_MASKS
    A = {n: nc.dram_tensor(f"in_{n}_dram", a.shape, mybir.dt.from_np(a.dtype), kind="ExternalInput").ap()
         for n, a in arrays.items()}
    out = nc.dram_tensor("out_0_dram", (1, T, D), F32, kind="ExternalOutput").ap()
    build(nc, A, out)
    r = run(nc, [{f"in_{n}_dram": a for n, a in arrays.items()}], core_ids=[0])
    return r.results[0]["out_0_dram"]
```
